# Optimizing a Trainium2 kernel written in Bass

```python
import jax, jax.numpy as jnp
from jax import lax
import numpy as np

D_MODEL = 1024
BATCH = 1
SEQ = 2048
DEPTH = 1

CHUNK = 64
N_META = 16

D_CONV = 512
CONV_K = 31
D_POOL = 512
POOL_WINDOWS = (2, 4, 8, 16)
N_POOL_GROUPS = len(POOL_WINDOWS)
POOL_GC = D_POOL // N_POOL_GROUPS
POOL_OUT = D_MODEL // N_POOL_GROUPS
D_SC = 512
SC_K = 3
N_BRANCH = 3
N_PROJ = 2 * D_CONV + D_POOL + 3 * D_SC + N_BRANCH * D_MODEL
SPLITS = tuple(int(s) for s in np.cumsum(
    [D_CONV, D_CONV, D_POOL, D_SC, D_SC, D_SC, D_MODEL, D_MODEL]))

N_GROUPS = 4
EXPERTS_PER_GROUP = 8
N_EXPERTS = N_GROUPS * EXPERTS_PER_GROUP
TOP_K = 2
D_EXPERT = 256
DISPATCH_BLOCK = 128

EPS = 1e-6

kernel_name = "hybrid_conv_pool_shortconv_hiermoe"

def rmsnorm(x, g):
    xf = x.astype(jnp.float32)
    y = xf * lax.rsqrt(jnp.mean(xf * xf, axis=-1, keepdims=True) + EPS)
    return (y * g.astype(jnp.float32)).astype(x.dtype)

def layernorm(x, g, b):
    xf = x.astype(jnp.float32)
    mu = jnp.mean(xf, axis=-1, keepdims=True)
    var = jnp.mean(jnp.square(xf - mu), axis=-1, keepdims=True)
    y = (xf - mu) * lax.rsqrt(var + EPS)
    return (y * g.astype(jnp.float32) + b.astype(jnp.float32)).astype(x.dtype)

def causal_dwconv(v, w):
    k, c = w.shape
    rhs = w[:, None, :].astype(v.dtype)
    return lax.conv_general_dilated(
        v, rhs, window_strides=(1,), padding=[(k - 1, 0)],
        dimension_numbers=("NWC", "WIO", "NWC"), feature_group_count=c)

def pool_mixer(v, pool_w, pool_scale):
    _, L, _ = v.shape
    vf = v.astype(jnp.float32)
    cs = jnp.cumsum(vf, axis=1)
    t = jnp.arange(L)
    outs = []
    for g, w in enumerate(POOL_WINDOWS):
        sl = slice(g * POOL_GC, (g + 1) * POOL_GC)
        csg = cs[..., sl]
        shifted = jnp.pad(csg[:, :L - w], ((0, 0), (w, 0), (0, 0)))
        cnt = jnp.minimum(t + 1, w).astype(jnp.float32)[:, None]
        outs.append((csg - shifted) / cnt - vf[..., sl])
    d = jnp.stack(outs, axis=2).astype(v.dtype)
    y = jnp.einsum("blgc,gcd->blgd", d, pool_w.astype(v.dtype))
    return y.reshape(v.shape[0], L, D_MODEL) * pool_scale.astype(v.dtype)

def hybrid_mixer(h, w_in, conv_w, conv_b, conv_ln_g, conv_ln_b, w_conv_out,
                 pool_w, pool_scale, sc_w, w_sc_out, w_out):
    proj = h @ w_in
    a_lin, a_gate, pb, cb, cc, cx, g_a, g_b, g_c = jnp.split(proj, SPLITS, axis=-1)
    u = a_lin * jax.nn.sigmoid(a_gate)
    u = causal_dwconv(u, conv_w) + conv_b.astype(u.dtype)
    u = layernorm(u, conv_ln_g, conv_ln_b)
    y_a = jax.nn.silu(u) @ w_conv_out
    y_b = pool_mixer(pb, pool_w, pool_scale)
    y_c = (cb * causal_dwconv(cc * cx, sc_w)) @ w_sc_out
    merged = jax.nn.sigmoid(g_a) * y_a + jax.nn.sigmoid(g_b) * y_b + jax.nn.sigmoid(g_c) * y_c
    return merged @ w_out

def hier_moe(h, w_group, b_group, w_router, b_router, w1, w3, w2):
    bsz, L, D = h.shape
    T = bsz * L
    hf = h.reshape(T, D)
    logit_g = (hf @ w_group).astype(jnp.float32) + b_group.astype(jnp.float32)
    p_g = jax.nn.softmax(logit_g, axis=-1)
    g_sel = jnp.argmax(logit_g, axis=-1)
    p_sel = jnp.take_along_axis(p_g, g_sel[:, None], axis=-1)
    logit_e = ((hf @ w_router).astype(jnp.float32) + b_router.astype(jnp.float32))
    logit_e = logit_e.reshape(T, N_GROUPS, EXPERTS_PER_GROUP)
    le = jnp.take_along_axis(logit_e, g_sel[:, None, None], axis=1)[:, 0]
    top_v, top_i = lax.top_k(le, TOP_K)
    w_tok = jax.nn.softmax(top_v, axis=-1) * p_sel
    expert_id = g_sel[:, None] * EXPERTS_PER_GROUP + top_i

    A = T * TOP_K
    flat_e = expert_id.reshape(A).astype(jnp.int32)
    flat_tok = jnp.repeat(jnp.arange(T, dtype=jnp.int32), TOP_K)
    flat_w = w_tok.reshape(A)
    order = jnp.argsort(flat_e)
    e_sorted = flat_e[order]
    counts = jnp.bincount(flat_e, length=N_EXPERTS).astype(jnp.int32)
    starts = jnp.cumsum(counts) - counts
    padded = ((counts + DISPATCH_BLOCK - 1) // DISPATCH_BLOCK) * DISPATCH_BLOCK
    pends = jnp.cumsum(padded)
    pstarts = pends - padded
    slot = pstarts[e_sorted] + (jnp.arange(A, dtype=jnp.int32) - starts[e_sorted])
    n_blocks = -(-A // DISPATCH_BLOCK) + N_EXPERTS
    P = n_blocks * DISPATCH_BLOCK
    buf_tok = jnp.zeros((P,), jnp.int32).at[slot].set(flat_tok[order])
    buf_w = jnp.zeros((P,), jnp.float32).at[slot].set(flat_w[order])
    block_start = jnp.arange(n_blocks, dtype=jnp.int32) * DISPATCH_BLOCK
    block_e = jnp.minimum(jnp.searchsorted(pends, block_start, side="right"), N_EXPERTS - 1)

    def run_block(args):
        tok, e = args
        xb = hf[tok]
        return (jax.nn.silu(xb @ w1[e]) * (xb @ w3[e])) @ w2[e]

    out = lax.map(run_block, (buf_tok.reshape(n_blocks, DISPATCH_BLOCK), block_e))
    out = out.reshape(P, D) * buf_w[:, None].astype(out.dtype)
    y = jax.ops.segment_sum(out, buf_tok, num_segments=T)
    return y.reshape(bsz, L, D)

def setup_inputs(seed: int = 0) -> dict:
    key = jax.random.key(seed)
    ks = jax.random.split(key, 24)

    def nrm(k, shape, scale):
        return jax.random.normal(k, shape, jnp.float32) * scale

    Ld = DEPTH
    return {
        "x": nrm(ks[0], (BATCH, SEQ, D_MODEL), 1.0),
        "meta": nrm(ks[1], (N_META, D_MODEL), 1.0),
        "norm_mix": 1.0 + nrm(ks[2], (Ld, D_MODEL), 0.02),
        "w_in": nrm(ks[3], (Ld, D_MODEL, N_PROJ), D_MODEL ** -0.5),
        "conv_w": nrm(ks[4], (Ld, CONV_K, D_CONV), CONV_K ** -0.5),
        "conv_b": nrm(ks[5], (Ld, D_CONV), 0.01),
        "conv_ln_g": 1.0 + nrm(ks[6], (Ld, D_CONV), 0.02),
        "conv_ln_b": nrm(ks[7], (Ld, D_CONV), 0.01),
        "w_conv_out": nrm(ks[8], (Ld, D_CONV, D_MODEL), D_CONV ** -0.5),
        "pool_w": nrm(ks[9], (Ld, N_POOL_GROUPS, POOL_GC, POOL_OUT), POOL_GC ** -0.5),
        "pool_scale": 1.0 + nrm(ks[10], (Ld, D_MODEL), 0.02),
        "sc_w": nrm(ks[11], (Ld, SC_K, D_SC), SC_K ** -0.5),
        "w_sc_out": nrm(ks[12], (Ld, D_SC, D_MODEL), D_SC ** -0.5),
        "w_out": nrm(ks[13], (Ld, D_MODEL, D_MODEL), D_MODEL ** -0.5),
        "norm_ffn": 1.0 + nrm(ks[14], (Ld, D_MODEL), 0.02),
        "w_group": nrm(ks[15], (Ld, D_MODEL, N_GROUPS), D_MODEL ** -0.5),
        "b_group": nrm(ks[16], (Ld, N_GROUPS), 0.01),
        "w_router": nrm(ks[17], (Ld, D_MODEL, N_EXPERTS), D_MODEL ** -0.5),
        "b_router": nrm(ks[18], (Ld, N_EXPERTS), 0.01),
        "w1": nrm(ks[19], (Ld, N_EXPERTS, D_MODEL, D_EXPERT), D_MODEL ** -0.5),
        "w3": nrm(ks[20], (Ld, N_EXPERTS, D_MODEL, D_EXPERT), D_MODEL ** -0.5),
        "w2": nrm(ks[21], (Ld, N_EXPERTS, D_EXPERT, D_MODEL), D_EXPERT ** -0.5),
        "final_norm": 1.0 + nrm(ks[22], (D_MODEL,), 0.02),
    }

def reference(x, meta, norm_mix, w_in, conv_w, conv_b, conv_ln_g, conv_ln_b, w_conv_out,
              pool_w, pool_scale, sc_w, w_sc_out, w_out, norm_ffn, w_group, b_group,
              w_router, b_router, w1, w3, w2, final_norm):
    bsz = x.shape[0]
    m = jnp.broadcast_to(meta.astype(x.dtype)[None], (bsz, N_META, D_MODEL))
    h = jnp.concatenate([m, x], axis=1)
    for l in range(DEPTH):
        h = h + hybrid_mixer(rmsnorm(h, norm_mix[l]), w_in[l], conv_w[l], conv_b[l],
                             conv_ln_g[l], conv_ln_b[l], w_conv_out[l], pool_w[l],
                             pool_scale[l], sc_w[l], w_sc_out[l], w_out[l])
        h = h + hier_moe(rmsnorm(h, norm_ffn[l]), w_group[l], b_group[l], w_router[l],
                         b_router[l], w1[l], w3[l], w2[l])
    h = rmsnorm(h, final_norm)
    return h[:, N_META:]


_drawn_inputs = setup_inputs


def setup_inputs(seed=0):
    import zlib

    import numpy as np

    out = dict(_drawn_inputs(seed))
    spreads = {}
    factors = {'conv_b': 4.215,
     'conv_ln_g': 14.109,
     'conv_ln_b': 29.204,
     'pool_scale': 12.084,
     'b_group': 26.002,
     'b_router': 17.223,
     'final_norm': 7.99,
     'norm_ffn': 4.274}
    for name, (base, spread) in spreads.items():
        noise = np.random.default_rng([zlib.crc32(name.encode()), seed]).standard_normal(out[name].shape)
        drawn = base * np.exp(spread * noise) if base else spread * noise
        out[name] = __import__('jax').numpy.asarray(drawn.astype(out[name].dtype))
    for name, factor in factors.items():
        out[name] = (out[name] * factor).astype(out[name].dtype)
    return out
```

```python
import concourse.bass as bass
from concourse import mybir
from concourse.alu_op_type import AluOpType as ALU
from contextlib import ExitStack

ACT = mybir.ActivationFunctionType
F32 = mybir.dt.float32
F32R = mybir.dt.float32r
I32 = mybir.dt.int32
U32 = mybir.dt.uint32

P = 128
D = 1024
KD = D // P
T = 2048
N_META = 16
CH = 4
TC = T // CH
PRE = 32
W = PRE + TC
WH = W // 2
DC = 512
KC = DC // P
CONV_K = 31
SC_K = 3
EPS = 1e-6
CREDIT = 16

A_LIN, A_GATE, POOL, SC_B, SC_C, SC_X, G_A, G_B, G_C = 0, 512, 1024, 1536, 2048, 2560, 3072, 4096, 5120

GA0, GC0, GP0, G10, G20, GROUPS = 0, 16, 36, 44, 76, 92
EA0, EC0, EP0, E10, E20, ACT_READS = 0, 16, 36, 44, 60, 68
V10, V20, DVE_READS = 0, 16, 24
S0 = dict(A=0, C=4, P=8, G1=10, G2=18, n=22)
S1 = dict(A=0, C=4, P=8, G1=10, G2=18, n=22)
S2 = dict(C=0, G2=4, n=8)
S3 = dict(G1=0, G2=8, n=12)
SLOT_K = (8, 8, 8, 5)
CONV_IN_A, CONV_IN_C = 13, 12
C_STEPS = 4 + CONV_IN_C
LN_STEPS, LN_ACTS = 19, 6
P_STEPS = 9


def three_products(pe, out, w_hi, w_lo, x_hi, x_lo, start, stop):
    pe.matmul(out, w_hi, x_hi, start=start, stop=False)
    pe.matmul(out, w_hi, x_lo, start=False, stop=False)
    return pe.matmul(out, w_lo, x_hi, start=False, stop=stop)


def setup(nc, ctx, ident, x, meta, w_in, pool_w, w_sc_out, norm_mix, conv_w, conv_b, conv_ln_g, conv_ln_b, pool_scale, sc_w,
          w_out, wo_raw, wo_loaded):
    def sb(name, shape, dt=F32):
        return ctx.enter_context(nc.sbuf_tensor(name, shape, dt))

    c = {}
    c["ident"] = ident
    c["mean_of"] = mean_of = sb("mean_of", [P, P])
    c["conv_taps"] = conv_taps = sb("conv_taps", [P, CONV_K, KC])
    c["chan"] = chan = sb("chan", [P, 32])
    c["g_mix"] = g_mix = sb("g_mix", [P, D])
    c["h_hi"] = h_hi = sb("h_hi", [P, KD, W], F32R)
    c["h_lo"] = h_lo = sb("h_lo", [P, KD, W], F32R)
    c["cx"] = cx = sb("cx", [P, 2 * KC, W])
    c["ms"] = ms = sb("ms", [P, 4])
    c["rstd"] = rstd = sb("rstd", [P, 4])
    c["raw"] = raw = [sb(f"raw{i}", [P, k, P]) for i, k in enumerate(SLOT_K)]
    c["raw_loaded"] = raw_loaded = [ctx.enter_context(nc.semaphore(f"raw_loaded{i}")) for i in range(4)]
    c["rows_loaded"] = rows_loaded = ctx.enter_context(nc.semaphore("rows_loaded"))
    c["rows"] = first_rows = cx[:, :, :].rearrange("p a b -> p (a b)")[:, 0:4 * D].rearrange("p (t n) -> p t n", t=4)
    with ExitStack() as inner:
        def scratch(name, shape):
            return inner.enter_context(nc.sbuf_tensor(name, shape, F32))[:, :]

        rows, rows2 = scratch("tap_rows", [P, P]), scratch("param_rows", [32, P])
        mrow, junk = scratch("meta_rows", [N_META, D]), scratch("meta_squares", [N_META, D])
        sem = lambda name: inner.enter_context(nc.semaphore(name))
        ps = inner.enter_context(nc.psum_tensor("ps_setup", [P, 8, 512], F32))
        loaded, gains, made, zeroed, sq, root, normed, moved, read = map(
            sem, ("loaded", "gains", "made", "zeroed", "sq", "root", "normed", "moved", "read"))
        block = inner.enter_context(nc.Block())

        @block.sync
        def _(sp):
            sp.dma_start(rows[0:CONV_K * KC, :], conv_w.rearrange("a k (c p) -> (a k c) p", p=P)).then_inc(loaded, 16)
            for at, src, n in ((0, conv_b, KC), (4, conv_ln_g, KC), (8, conv_ln_b, KC), (12, pool_scale, KD)):
                sp.dma_start(rows2[at:at + n, :], src.rearrange("a (c p) -> (a c) p", p=P)).then_inc(loaded, 16)
            sp.dma_start(rows2[20:32, :], sc_w.rearrange("a k (c p) -> (a k c) p", p=P)).then_inc(loaded, 16)
            sp.dma_start(mrow, meta).then_inc(loaded, 16)
            sp.dma_start(g_mix[:, :], norm_mix.to_broadcast([P, D])).then_inc(gains, 16)
            sp.dma_start(first_rows, x.rearrange("b (t p) n -> p (b t) n", p=P)[:, 0:4, :]).then_inc(rows_loaded, 16)

            def tile_of(w, first):
                return w.rearrange("a (k p) n -> p (a k) n", p=P)[:, :, first:first + P]

            for slot, first in ((0, A_LIN), (1, A_GATE), (2, SC_X)):
                sp.dma_start(raw[slot][:, :, :], tile_of(w_in, first)).then_inc(raw_loaded[slot], 16)
            sp.dma_start(raw[3][:, 0:1, :], pool_w.rearrange("a g p n -> p (a g) n")[:, 0:1, 0:P]).then_inc(raw_loaded[3], 16)
            sp.dma_start(raw[3][:, 1:1 + KC, :], tile_of(w_sc_out, 0)).then_inc(raw_loaded[3], 16)
            for k in range(2):
                sp.dma_start(wo_raw[:, k, :], w_out.rearrange("a (k p) n -> p (a k) n", p=P)[:, k, :]).then_inc(wo_loaded[k], 16)

        @block.gpsimd
        def _(pool):
            pool.memset(ident[:, :], 0.0).then_inc(made, 1)
            pool.memset(mean_of[:, :], 1.0 / DC).then_inc(made, 1)
            pool.wait_ge(made, 1)
            pool.affine_select(out=ident[:, :], in_=ident[:, :], compare_op=ALU.not_equal, fill=1.0,
                               base=0, pattern=[[-1, P]], channel_multiplier=1).then_inc(made, 1)

        @block.scalar
        def _(act):
            act.wait_ge(loaded, 7 * 16)
            act.activation(junk, mrow, ACT.Square, accum_out=ms[0:N_META, 0:1]).then_inc(sq, 1)
            act.wait_ge(sq, 2)
            act.activation(ms[0:N_META, 2:3], ms[0:N_META, 1:2], ACT.Sqrt).then_inc(root, 1)

        @block.vector
        def _(dve):
            dve.memset(h_hi[:, :, TC:W].bitcast(F32), 0.0)
            dve.memset(h_lo[:, :, TC:W].bitcast(F32), 0.0).then_inc(zeroed, 1)
            dve.wait_ge(sq, 1)
            dve.tensor_scalar(ms[0:N_META, 1:2], ms[0:N_META, 0:1], 1.0 / D, EPS, ALU.mult, ALU.add).then_inc(sq, 1)
            dve.wait_ge(root, 1)
            dve.reciprocal(rstd[0:N_META, 0:1], ms[0:N_META, 2:3]).then_inc(root, 1)
            dve.wait_ge(root, 2)
            dve.wait_ge(gains, 16)
            dve.scalar_tensor_tensor(out=mrow, in0=mrow, scalar=rstd[0:N_META, 0:1],
                                     in1=g_mix[0:N_META, :],
                                     op0=ALU.mult, op1=ALU.mult).then_inc(normed, 1)
            dve.wait_ge(moved, 1)
            dve.tensor_copy(conv_taps[:, :, :], ps[:, 0, 0:CONV_K * KC].rearrange("p (k c) -> p k c", c=KC))
            dve.tensor_copy(chan[:, :], ps[:, 1, 0:32])
            dve.wait_ge(zeroed, 1)
            meta_cols = ps[:, 2, 0:KD * N_META].rearrange("p (k m) -> p k m", m=N_META)
            dve.tensor_copy(h_hi[:, :, W - N_META:W], meta_cols).then_inc(read, 1)
            dve.wait_ge(read, 1)
            dve.tensor_tensor(h_lo[:, :, W - N_META:W], meta_cols, h_hi[:, :, W - N_META:W].bitcast(F32),
                              ALU.subtract).then_inc(read, 1)

        @block.tensor
        def _(pe):
            pe.wait_ge(loaded, 7 * 16)
            pe.wait_ge(made, 3)
            n = CONV_K * KC
            pe.transpose(ps[:, 0, 0:n], rows[0:n, :], ident[0:n, 0:n])
            pe.transpose(ps[:, 1, 0:32], rows2, ident[0:32, 0:32])
            pe.wait_ge(normed, 1)
            for k in range(KD):
                src = mrow[:, k * P:(k + 1) * P]
                last = pe.transpose(ps[:, 2, k * N_META:(k + 1) * N_META], src, ident[0:N_META, 0:N_META])
            last.then_inc(moved, 1)
    return c


def mixer(nc, c, x, w_in, w_conv_out, pool_w, w_sc_out, merged):
    ident, mean_of, conv_taps, chan, g_mix = c["ident"], c["mean_of"], c["conv_taps"], c["chan"], c["g_mix"]
    h_hi, h_lo, cx, ms, rstd = c["h_hi"], c["h_lo"], c["cx"], c["ms"], c["rstd"]
    ctx = ExitStack()
    with ctx:
        def sb(name, shape, dt=F32):
            return ctx.enter_context(nc.sbuf_tensor(name, shape, dt))

        def sem(name):
            return ctx.enter_context(nc.semaphore(name))

        u = sb("u", [P, KC, W])
        acc = sb("acc", [P, KC, TC])
        sa_hi, sa_lo = sb("sa_hi", [P, KC, TC], F32R), sb("sa_lo", [P, KC, TC], F32R)
        sc_hi, sc_lo = sb("sc_hi", [P, KC, TC], F32R), sb("sc_lo", [P, KC, TC], F32R)
        d_hi, d_lo = sb("d_hi", [P, KC, TC], F32R), sb("d_lo", [P, KC, TC], F32R)
        m = sb("m", [P, 2 * KC, W])
        rows, raw = c["rows"], c["raw"]
        sg = sb("sg", [P, W])
        gates = sb("gates", [P, 4, TC])
        w_hi = [sb(f"w_hi{i}", [P, k, P], F32R) for i, k in enumerate(SLOT_K)]
        w_lo = [sb(f"w_lo{i}", [P, k, P], F32R) for i, k in enumerate(SLOT_K)]
        tmp = sb("tmp", [P, 2, TC])
        stat = sb("stat", [P, TC])
        ps = ctx.enter_context(nc.psum_tensor("ps_mix", [P, 8, 512], F32))

        raw_loaded, rows_loaded = c["raw_loaded"], c["rows_loaded"]
        hi_made = [sem(f"hi_made{i}") for i in range(4)]
        w_ready = [sem(f"w_ready{i}") for i in range(4)]
        waited = sem("waited")
        squares, rows_root, rows_step, rows_normed = map(
            sem, ("squares", "rows_root", "rows_step", "rows_normed"))
        turned, h_hi_made, h_ready, context_kept = map(sem, ("turned", "h_hi_made", "h_ready", "context_kept"))
        group_done, act_read, dve_read = map(sem, ("group_done", "act_read", "dve_read"))
        u_ready, a_step, c_step, conv_step, p_step, ln_step = map(
            sem, ("u_ready", "a_step", "c_step", "conv_step", "p_step", "ln_step"))
        sc_ready, d_ready, sa_ready, sum_ready, stat_done, ln_act = map(
            sem, ("sc_ready", "d_ready", "sa_ready", "sum_ready", "stat_done", "ln_act"))
        m_step, merged_ready, merged_stored = map(sem, ("m_step", "merged_ready", "merged_stored"))
        block = ctx.enter_context(nc.Block())

        w_in_v = w_in.rearrange("a (k p) n -> p (a k) n", p=P)
        conv_out_v = w_conv_out.rearrange("a (k p) n -> p (a k) n", p=P)
        sc_out_v = w_sc_out.rearrange("a (k p) n -> p (a k) n", p=P)
        pool_v = pool_w.rearrange("a g p n -> p (a g) n")
        x_v = x.rearrange("b (t p) n -> p (b t) n", p=P)
        merged_v = merged.rearrange("j p t -> p j t")

        @block.sync
        def _(sp):
            def load(slot, n, *pieces):
                sp.wait_ge(w_ready[slot], n + CREDIT)
                if slot == 2:
                    sp.sem_inc(waited, 1)
                at = 0
                for src, k in pieces:
                    sp.dma_start(raw[slot][:, at:at + k, :], src).then_inc(raw_loaded[slot], 16)
                    at += k

            def w_in_at(first):
                return w_in_v[:, :, bass.ds(first, P)], KD

            def sc_out_at(first):
                return sc_out_v[:, :, bass.ds(first, P)], KC

            def conv_out_at(first):
                return conv_out_v[:, :, bass.ds(first, P)], KC

            def conv_out_halves(first):
                return ((conv_out_v[:, 0:2, bass.ds(first, P)], 2), (conv_out_v[:, 2:4, bass.ds(first, P)], 2))

            for s in w_ready:
                sp.sem_inc(s, CREDIT)
            with sp.Fori(0, CH) as ch:
                n0, n1, n2, n3 = ch * S0["n"], ch * S1["n"], ch * S2["n"], ch * S3["n"]
                with sp.Fori(1, KC) as i:
                    load(0, n0 + i + S0["A"], w_in_at(i * P + A_LIN))
                    load(1, n1 + i + S1["A"], w_in_at(i * P + A_GATE))
                load(0, n0 + S0["C"], w_in_at(SC_B))
                load(1, n1 + S1["C"], w_in_at(SC_C))
                with sp.Fori(1, KC) as i:
                    load(0, n0 + i + S0["C"], w_in_at(i * P + SC_B))
                    load(1, n1 + i + S1["C"], w_in_at(i * P + SC_C))
                    load(2, n2 + i + S2["C"], w_in_at(i * P + SC_X))
                load(0, n0 + S0["P"], w_in_at(POOL))
                load(1, n1 + S1["P"], w_in_at(POOL + P))
                load(2, n2 + S2["G2"], conv_out_at(0))
                load(0, n0 + S0["P"] + 1, w_in_at(POOL + 2 * P))
                load(1, n1 + S1["P"] + 1, w_in_at(POOL + 3 * P))
                load(0, n0 + S0["G1"], w_in_at(G_B))
                load(1, n1 + S1["G1"], w_in_at(G_C))
                with sp.Fori(0, KC - 1) as g:
                    for jj in (1, 2):
                        load(0, n0 + g * 2 + (S0["G1"] + jj), w_in_at(g * 2 * P + (G_B + jj * P)))
                        load(1, n1 + g * 2 + (S1["G1"] + jj), w_in_at(g * 2 * P + (G_C + jj * P)))
                        load(3, n3 + g * 2 + (S3["G1"] + jj),
                             (pool_v[:, bass.ds(g + jj // 2, 1), (jj % 2) * P:(jj % 2 + 1) * P], 1),
                             sc_out_at(g * 2 * P + jj * P))
                load(0, n0 + S0["G1"] + 7, w_in_at(G_B + 7 * P))
                load(1, n1 + S1["G1"] + 7, w_in_at(G_C + 7 * P))
                load(3, n3 + S3["G1"] + 7, (pool_v[:, KC - 1:KC, P:2 * P], 1), sc_out_at(7 * P))
                load(0, n0 + S0["G2"], w_in_at(G_A))
                load(1, n1 + S1["G2"], w_in_at(G_A + P))
                load(3, n3 + S3["G2"], *conv_out_halves(P))
                sp.wait_ge(d_ready, ch + 1)
                sp.sem_inc(waited, 1)
                sp.dma_start(rows, x_v[:, bass.ds(((ch + 1) & (CH - 1)) * 4, 4), :]).then_inc(rows_loaded, 16)
                with sp.Fori(1, KC) as i:
                    load(0, n0 + i + S0["G2"], w_in_at(i * 2 * P + G_A))
                    load(2, n2 + i + S2["G2"], conv_out_at(i * 2 * P))
                    load(1, n1 + i + S1["G2"], w_in_at(i * 2 * P + (G_A + P)))
                    load(3, n3 + i + S3["G2"], *conv_out_halves(i * 2 * P + P))
                load(0, n0 + S0["n"], w_in_at(A_LIN))
                load(2, n2 + S2["n"], w_in_at(SC_X))
                load(1, n1 + S1["n"], w_in_at(A_GATE))
                load(3, n3 + S3["n"], (pool_v[:, 0:1, 0:P], 1), sc_out_at(0))

        @block.scalar
        def _(act):
            def split(slot, n, uses):
                act.wait_ge(raw_loaded[slot], n * uses + uses)
                act.copy(w_hi[slot][:, :, :], raw[slot][:, :, :]).then_inc(hi_made[slot], 1)

            def read(out, bank, width, done, func=None):
                act.wait_ge(group_done, done)
                of = ps[:, bank, 0:width]
                (act.activation(out, of, func) if func else act.copy(out, of)).then_inc(act_read, 1)

            def root_mean_square(n):
                act.wait_ge(rows_loaded, n * 16 + 16)
                for t in range(4):
                    act.activation(ps[:, 4:6, :], rows[:, t, :].rearrange("p (a n) -> p a n", a=2), ACT.Square,
                                   accum_out=ms[:, t:t + 1]).then_inc(squares, 1)
                    act.wait_ge(squares, n * 5 + (t + 1))
                act.wait_ge(squares, n * 5 + 5)
                act.activation(ms[:, :], ms[:, :], ACT.Sqrt).then_inc(rows_root, 1)

            act.sem_inc(act_read, CREDIT)
            act.sem_inc(merged_stored, CREDIT)
            root_mean_square(0)
            for slot, size in ((0, 16), (1, 16), (2, 16), (3, 32)):
                split(slot, 0, size)
            with act.Fori(0, CH) as ch:
                act.wait_ge(context_kept, ch + 1)
                for t in range(4):
                    for q in range(2):
                        act.wait_ge(turned, ch * 8 + (2 * t + q + 1))
                        act.copy(h_hi[:, q * 4:q * 4 + 4, PRE + t * P:PRE + (t + 1) * P],
                                 ps[:, 4 + 2 * (t % 2) + q, :].rearrange("p (k n) -> p k n", n=P)).then_inc(h_hi_made, 1)
                with act.Fori(0, KC) as i:
                    at = ch * GROUPS + i * 4 + (GA0 + CREDIT)
                    read(u[:, i, 0:WH], 0, WH, at + 1)
                    read(u[:, i, WH:W], 1, WH, at + 2)
                    split(0, ch * S0["n"] + i + (S0["A"] + 1), 16)
                    act.wait_ge(u_ready, ch * KC + i + CREDIT)
                    read(sg[:, 0:WH], 2, WH, at + 3, ACT.Sigmoid)
                    read(sg[:, WH:W], 3, WH, at + 4, ACT.Sigmoid)
                    split(1, ch * S1["n"] + i + (S1["A"] + 1), 16)
                act.wait_ge(merged_stored, ch * 16 + CREDIT)
                with act.Fori(0, KC) as i:
                    at = ch * GROUPS + i * 5 + (GC0 + CREDIT)
                    read(m[:, i, PRE:W], 4, TC, at + 1)
                    split(0, ch * S0["n"] + i + (S0["C"] + 1), 16)
                    read(cx[:, i, 0:WH], 0, WH, at + 2)
                    read(cx[:, i, WH:W], 1, WH, at + 3)
                    split(1, ch * S1["n"] + i + (S1["C"] + 1), 16)
                    read(cx[:, i + KC, 0:WH], 2, WH, at + 4)
                    read(cx[:, i + KC, WH:W], 3, WH, at + 5)
                    split(2, ch * S2["n"] + i + (S2["C"] + 1), 16)
                with act.Fori(0, 2) as i:
                    at = ch * GROUPS + i * 4 + (GP0 + CREDIT)
                    read(m[:, i * 2 + KC, 0:WH], 0, WH, at + 1)
                    read(m[:, i * 2 + KC, WH:W], 1, WH, at + 2)
                    split(0, ch * S0["n"] + i + (S0["P"] + 1), 16)
                    read(m[:, i * 2 + (KC + 1), 0:WH], 2, WH, at + 3)
                    read(m[:, i * 2 + (KC + 1), WH:W], 3, WH, at + 4)
                    split(1, ch * S1["n"] + i + (S1["P"] + 1), 16)

                def g1_pass(g):
                    for jj in range(2):
                        at = ch * GROUPS + g * 8 + (G10 + jj * 4 + CREDIT)
                        act.wait_ge(dve_read, ch * DVE_READS + g * 4 + (V10 + jj * 2 - 2 + CREDIT))
                        read(gates[:, jj * 2, :], 0, TC, at + 1, ACT.Sigmoid)
                        split(0, ch * S0["n"] + g * 2 + (S0["G1"] + jj + 1), 16)
                        read(gates[:, jj * 2 + 1, :], 1, TC, at + 2, ACT.Sigmoid)
                        split(1, ch * S1["n"] + g * 2 + (S1["G1"] + jj + 1), 16)
                        act.wait_ge(group_done, at + 4)
                        split(3, ch * S3["n"] + g * 2 + (S3["G1"] + jj + 1), 32)

                g1_pass(0)
                act.wait_ge(ln_step, ch * LN_STEPS + 6)
                act.activation(u[:, :, 0:TC], acc[:, :, :], ACT.Square).then_inc(ln_act, 1)
                g1_pass(1)
                act.wait_ge(ln_step, ch * LN_STEPS + 8)
                act.activation(stat[:, :], stat[:, :], ACT.Sqrt).then_inc(ln_act, 1)
                for k in range(KC):
                    act.wait_ge(ln_step, ch * LN_STEPS + (10 + k))
                    act.activation(u[:, k, 0:TC], acc[:, k, :], ACT.Sigmoid, bias=chan[:, 8 + k:9 + k]).then_inc(ln_act, 1)
                with act.Fori(2, KC) as g:
                    g1_pass(g)
                act.wait_ge(dve_read, ch * DVE_READS + (V20 + CREDIT))
                root_mean_square(ch + 1)
                with act.Fori(0, KC) as i:
                    at = ch * GROUPS + i * 4 + (G20 + CREDIT)
                    act.wait_ge(dve_read, ch * DVE_READS + i * 2 + (V20 - 1 + CREDIT))
                    read(gates[:, 0, :], 0, TC, at + 1, ACT.Sigmoid)
                    split(0, ch * S0["n"] + i + (S0["G2"] + 1), 16)
                    act.wait_ge(group_done, at + 2)
                    split(2, ch * S2["n"] + i + (S2["G2"] + 1), 16)
                    act.wait_ge(dve_read, ch * DVE_READS + i * 2 + (V20 + CREDIT))
                    read(gates[:, 2, :], 1, TC, at + 3, ACT.Sigmoid)
                    split(1, ch * S1["n"] + i + (S1["G2"] + 1), 16)
                    act.wait_ge(group_done, at + 4)
                    split(3, ch * S3["n"] + i + (S3["G2"] + 1), 32)
                act.wait_ge(merged_ready, ch * 2 * KC + 2 * KC)
                act.dma_start(merged_v[:, :, bass.ds(ch * TC, TC)], m[:, :, PRE:W]).then_inc(merged_stored, 16)
            act.wait_ge(merged_stored, CH * 16 + CREDIT)

        @block.gpsimd
        def _(pool):
            def split(slot, n):
                pool.wait_ge(hi_made[slot], n + 1)
                pool.tensor_tensor(w_lo[slot][:, :, :], raw[slot][:, :, :], w_hi[slot][:, :, :].bitcast(F32),
                                   ALU.subtract).then_inc(w_ready[slot], 1)

            for slot in range(4):
                split(slot, 0)
            with pool.Fori(0, CH) as ch:
                with pool.Fori(0, KC) as i:
                    split(0, ch * S0["n"] + i + (S0["A"] + 1))
                    split(1, ch * S1["n"] + i + (S1["A"] + 1))
                with pool.Fori(0, KC) as i:
                    split(0, ch * S0["n"] + i + (S0["C"] + 1))
                    split(1, ch * S1["n"] + i + (S1["C"] + 1))
                    split(2, ch * S2["n"] + i + (S2["C"] + 1))
                with pool.Fori(0, 2) as i:
                    split(0, ch * S0["n"] + i + (S0["P"] + 1))
                    split(1, ch * S1["n"] + i + (S1["P"] + 1))
                with pool.Fori(0, 2 * KC) as j:
                    split(0, ch * S0["n"] + j + (S0["G1"] + 1))
                    split(1, ch * S1["n"] + j + (S1["G1"] + 1))
                    split(3, ch * S3["n"] + j + (S3["G1"] + 1))
                with pool.Fori(0, KC) as i:
                    split(0, ch * S0["n"] + i + (S0["G2"] + 1))
                    split(2, ch * S2["n"] + i + (S2["G2"] + 1))
                    split(1, ch * S1["n"] + i + (S1["G2"] + 1))
                    split(3, ch * S3["n"] + i + (S3["G2"] + 1))

        @block.vector
        def _(dve):
            def norm_rows(n):
                dve.wait_ge(squares, n * 5 + 4)
                dve.tensor_scalar(ms[:, :], ms[:, :], 1.0 / D, EPS, ALU.mult, ALU.add).then_inc(squares, 1)
                dve.wait_ge(rows_root, n + 1)
                dve.reciprocal(rstd[:, :], ms[:, :]).then_inc(rows_step, 1)
                dve.wait_ge(rows_step, n + 1)
                for t in range(4):
                    dve.scalar_tensor_tensor(out=rows[:, t, :], in0=rows[:, t, :], scalar=rstd[:, t:t + 1],
                                             in1=g_mix[:, :], op0=ALU.mult, op1=ALU.mult).then_inc(rows_normed, 1)

            def tap(i, k, s, done):
                src = u[:, i, PRE - (CONV_K - 1) + k:PRE - (CONV_K - 1) + k + TC]
                if k == 0:
                    dve.tensor_scalar(acc[:, i, :], src, conv_taps[:, k, bass.ds(i, 1)], chan[:, bass.ds(i, 1)],
                                      ALU.mult, ALU.add).then_inc(s, 1)
                else:
                    dve.wait_ge(s, done)
                    dve.scalar_tensor_tensor(out=acc[:, i, :], in0=src, scalar=conv_taps[:, k, bass.ds(i, 1)],
                                             in1=acc[:, i, :], op0=ALU.mult, op1=ALU.add).then_inc(s, 1)

            dve.sem_inc(u_ready, CREDIT)
            dve.sem_inc(dve_read, CREDIT)
            norm_rows(0)
            with dve.Fori(0, CH) as ch:
                dve.wait_ge(group_done, ch * GROUPS + CREDIT)
                dve.tensor_copy(h_hi[:, :, 0:PRE], h_hi[:, :, TC:W].bitcast(F32))
                dve.tensor_copy(h_lo[:, :, 0:PRE], h_lo[:, :, TC:W].bitcast(F32)).then_inc(context_kept, 1)
                dve.wait_ge(context_kept, ch + 1)
                for t in range(4):
                    for q in range(2):
                        at = h_hi[:, q * 4:q * 4 + 4, PRE + t * P:PRE + (t + 1) * P]
                        dve.wait_ge(h_hi_made, ch * 8 + (2 * t + q + 1))
                        dve.tensor_tensor(h_lo[:, q * 4:q * 4 + 4, PRE + t * P:PRE + (t + 1) * P],
                                          ps[:, 4 + 2 * (t % 2) + q, :].rearrange("p (k n) -> p k n", n=P),
                                          at.bitcast(F32), ALU.subtract).then_inc(h_ready, 1)
                with dve.Fori(0, KC) as i:
                    dve.wait_ge(act_read, ch * ACT_READS + i * 4 + (EA0 + 4 + CREDIT))
                    dve.tensor_tensor(u[:, i, :], u[:, i, :], sg[:, :], ALU.mult).then_inc(u_ready, 1)
                    dve.wait_ge(u_ready, ch * KC + i + (1 + CREDIT))
                    for k in range(CONV_IN_A):
                        tap(i, k, a_step, ch * KC * CONV_IN_A + i * CONV_IN_A + k)
                with dve.Fori(0, KC) as i:
                    base = ch * KC * C_STEPS + i * C_STEPS
                    v = cx[:, i, :]
                    dve.wait_ge(a_step, ch * KC * CONV_IN_A + KC * CONV_IN_A)
                    dve.wait_ge(act_read, ch * ACT_READS + i * 5 + (EC0 + 5 + CREDIT))
                    dve.tensor_tensor(v, v, cx[:, i + KC, :], ALU.mult).then_inc(c_step, 1)
                    dve.wait_ge(c_step, base + 1)
                    dve.tensor_scalar(tmp[:, 0, :], cx[:, i, PRE - 2:W - 2], chan[:, bass.ds(i + 20, 1)], None,
                                      ALU.mult).then_inc(c_step, 1)
                    for k in (1, 2):
                        dve.wait_ge(c_step, base + (k + 1))
                        dve.scalar_tensor_tensor(out=tmp[:, 0, :], in0=cx[:, i, PRE - 2 + k:W - 2 + k],
                                                 scalar=chan[:, bass.ds(i + (20 + k * KC), 1)], in1=tmp[:, 0, :],
                                                 op0=ALU.mult, op1=ALU.add).then_inc(c_step, 1)
                    dve.wait_ge(c_step, base + 4)
                    dve.tensor_tensor(tmp[:, 1, :], tmp[:, 0, :], m[:, i, PRE:W], ALU.mult).then_inc(sc_ready, 1)
                    dve.wait_ge(sc_ready, ch * 3 * KC + i * 3 + 1)
                    dve.tensor_copy(sc_hi[:, i, :], tmp[:, 1, :]).then_inc(sc_ready, 1)
                    dve.wait_ge(sc_ready, ch * 3 * KC + i * 3 + 2)
                    dve.tensor_tensor(sc_lo[:, i, :], tmp[:, 1, :], sc_hi[:, i, :].bitcast(F32),
                                      ALU.subtract).then_inc(sc_ready, 1)
                    for n in range(CONV_IN_C):
                        tap(i, CONV_IN_A + n, c_step, base + (4 + n))
                pb, s_a, s_b = m[:, KC:2 * KC, :], cx[:, KC:2 * KC, :], cx[:, 0:KC, :]
                base = ch * P_STEPS
                dve.wait_ge(act_read, ch * ACT_READS + (E10 + CREDIT))
                dve.wait_ge(c_step, ch * KC * C_STEPS + KC * C_STEPS)
                dve.wait_ge(sc_ready, ch * 3 * KC + 3 * KC)
                dve.tensor_tensor(s_a[:, :, 17:W], pb[:, :, 17:W], pb[:, :, 16:W - 1], ALU.add).then_inc(p_step, 1)
                dve.wait_ge(p_step, base + 1)
                dve.tensor_tensor(s_b[:, 1:4, 19:W], s_a[:, 1:4, 19:W], s_a[:, 1:4, 17:W - 2], ALU.add).then_inc(p_step, 1)
                dve.wait_ge(p_step, base + 2)
                dve.tensor_tensor(s_a[:, 2:4, 23:W], s_b[:, 2:4, 23:W], s_b[:, 2:4, 19:W - 4], ALU.add).then_inc(p_step, 1)
                dve.wait_ge(p_step, base + 3)
                dve.tensor_tensor(s_b[:, 3, 31:W], s_a[:, 3, 31:W], s_a[:, 3, 23:W - 8], ALU.add).then_inc(p_step, 1)
                dve.wait_ge(p_step, base + 4)
                for g, s in enumerate((s_a, s_b, s_a, s_b)):
                    dve.scalar_tensor_tensor(out=s_b[:, g, PRE:W], in0=s[:, g, PRE:W], scalar=1.0 / 2 ** (g + 1),
                                             in1=pb[:, g, PRE:W], op0=ALU.mult, op1=ALU.subtract).then_inc(p_step, 1)
                dve.wait_ge(p_step, base + 8)
                dve.tensor_copy(d_hi[:, :, :], s_b[:, :, PRE:W]).then_inc(p_step, 1)
                dve.wait_ge(p_step, base + 9)
                dve.tensor_tensor(d_lo[:, :, :], s_b[:, :, PRE:W], d_hi[:, :, :].bitcast(F32),
                                  ALU.subtract).then_inc(d_ready, 1)
                rest = CONV_K - CONV_IN_A - CONV_IN_C
                for n in range(rest):
                    for i in range(KC):
                        tap(i, CONV_IN_A + CONV_IN_C + n, conv_step, ch * rest * KC + (max(n * KC + i - KC + 1, 0)))
                base = ch * LN_STEPS
                dve.wait_ge(conv_step, ch * rest * KC + rest * KC)
                dve.tensor_tensor(u[:, 0:2, 0:TC], acc[:, 0:2, :], acc[:, 2:4, :], ALU.add).then_inc(ln_step, 1)
                dve.wait_ge(ln_step, base + 1)
                dve.tensor_tensor(u[:, 2, 0:TC], u[:, 0, 0:TC], u[:, 1, 0:TC], ALU.add).then_inc(ln_step, 1)

                def g1_pass(g):
                    for jj in range(2):
                        n = ch * 2 * KC + g * 2 + jj
                        out = m[:, g * 2 + jj, PRE:W]
                        dve.wait_ge(group_done, ch * GROUPS + g * 8 + (G10 + jj * 4 + 3 + CREDIT))
                        dve.wait_ge(act_read, ch * ACT_READS + g * 4 + (E10 + jj * 2 + 2 + CREDIT))
                        dve.scalar_tensor_tensor(out=out, in0=ps[:, 2 + 2 * jj, :],
                                                 scalar=chan[:, bass.ds(g * 2 + (12 + jj), 1)],
                                                 in1=gates[:, jj * 2, :], op0=ALU.mult, op1=ALU.mult).then_inc(dve_read, 1)
                        dve.wait_ge(group_done, ch * GROUPS + g * 8 + (G10 + jj * 4 + 4 + CREDIT))
                        dve.tensor_tensor(tmp[:, jj, :], ps[:, 3 + 2 * jj, :], gates[:, jj * 2 + 1, :],
                                          ALU.mult).then_inc(dve_read, 1)
                        dve.wait_ge(dve_read, ch * DVE_READS + g * 4 + (V10 + jj * 2 + 2 + CREDIT))
                        dve.tensor_tensor(out, out, tmp[:, jj, :], ALU.add).then_inc(m_step, 1)

                g1_pass(0)
                dve.wait_ge(stat_done, ch * 2 + 1)
                for k in range(KC):
                    dve.tensor_tensor(acc[:, k, :], acc[:, k, :], ps[:, 6, :], ALU.subtract).then_inc(ln_step, 1)
                dve.wait_ge(ln_act, ch * LN_ACTS + 1)
                dve.tensor_tensor(u[:, 0:2, 0:TC], u[:, 0:2, 0:TC], u[:, 2:4, 0:TC], ALU.add).then_inc(ln_step, 1)
                dve.wait_ge(ln_step, base + 7)
                dve.tensor_tensor(u[:, 2, 0:TC], u[:, 0, 0:TC], u[:, 1, 0:TC], ALU.add).then_inc(sum_ready, 1)
                g1_pass(1)
                dve.wait_ge(stat_done, ch * 2 + 2)
                dve.tensor_scalar(stat[:, :], ps[:, 7, :], EPS, None, ALU.add).then_inc(ln_step, 1)
                dve.wait_ge(ln_act, ch * LN_ACTS + 2)
                dve.reciprocal(stat[:, :], stat[:, :]).then_inc(ln_step, 1)
                dve.wait_ge(ln_step, base + 9)
                for k in range(KC):
                    dve.scalar_tensor_tensor(out=acc[:, k, :], in0=acc[:, k, :], scalar=chan[:, 4 + k:5 + k],
                                             in1=stat[:, :], op0=ALU.mult, op1=ALU.mult).then_inc(ln_step, 1)
                for k in range(KC):
                    dve.wait_ge(ln_act, ch * LN_ACTS + (3 + k))
                    dve.scalar_tensor_tensor(out=acc[:, k, :], in0=acc[:, k, :], scalar=chan[:, 8 + k:9 + k],
                                             in1=u[:, k, 0:TC], op0=ALU.add, op1=ALU.mult).then_inc(ln_step, 1)
                dve.wait_ge(ln_step, base + 17)
                dve.tensor_copy(sa_hi[:, :, :], acc[:, :, :]).then_inc(ln_step, 1)
                dve.wait_ge(ln_step, base + 18)
                dve.tensor_tensor(sa_lo[:, :, :], acc[:, :, :], sa_hi[:, :, :].bitcast(F32),
                                  ALU.subtract).then_inc(ln_step, 1)
                with dve.Fori(2, KC) as g:
                    g1_pass(g)
                norm_rows(ch + 1)
                with dve.Fori(0, KC) as i:
                    for jj in range(2):
                        out = m[:, i * 2 + jj, PRE:W]
                        dve.wait_ge(group_done, ch * GROUPS + i * 4 + (G20 + jj * 2 + 2 + CREDIT))
                        dve.wait_ge(act_read, ch * ACT_READS + i * 2 + (E20 + jj + 1 + CREDIT))
                        dve.wait_ge(m_step, ch * 2 * KC + 2 * KC)
                        dve.tensor_tensor(tmp[:, jj, :], ps[:, 2 + jj, :], gates[:, 2 * jj, :],
                                          ALU.mult).then_inc(dve_read, 1)
                        dve.wait_ge(dve_read, ch * DVE_READS + i * 2 + (V20 + jj + 1 + CREDIT))
                        dve.tensor_tensor(out, out, tmp[:, jj, :], ALU.add).then_inc(merged_ready, 1)

        @block.tensor
        def _(pe):
            def group(bank, width, slot, k0, ks, hi, lo, first=0):
                out = ps[:, bank, 0:width]
                for k in range(ks):
                    last = three_products(pe, out, w_hi[slot][:, k0 + k, :], w_lo[slot][:, k0 + k, :],
                                          hi[:, k, first:first + width], lo[:, k, first:first + width],
                                          k == 0, k == ks - 1)
                last.then_inc(group_done, 1)

            def tile_with_context(slot, banks, free):
                for q in range(2):
                    pe.wait_ge(act_read, free + q)
                    group(banks + q, WH, slot, 0, KD, h_hi, h_lo, q * WH)

            pe.sem_inc(group_done, CREDIT)
            with pe.Fori(0, CH) as ch:
                pe.wait_ge(dve_read, ch * DVE_READS + CREDIT)
                for t in range(4):
                    pe.wait_ge(rows_normed, ch * 4 + (t + 1))
                    for q in range(2):
                        if t >= 2:
                            pe.wait_ge(h_ready, ch * 8 + (2 * (t - 2) + q + 1))
                        for k in range(4):
                            last = pe.transpose(ps[:, 4 + 2 * (t % 2) + q, k * P:(k + 1) * P],
                                                rows[:, t, (4 * q + k) * P:(4 * q + k + 1) * P], ident[:, :])
                        last.then_inc(turned, 1)
                with pe.Fori(0, KC) as i:
                    pe.wait_ge(h_ready, ch * 8 + 8)
                    free = ch * ACT_READS + i * 4 + (EA0 + CREDIT)
                    pe.wait_ge(w_ready[0], ch * S0["n"] + i + (S0["A"] + 1 + CREDIT))
                    tile_with_context(0, 0, free - 1)
                    pe.wait_ge(w_ready[1], ch * S1["n"] + i + (S1["A"] + 1 + CREDIT))
                    tile_with_context(1, 2, free - 1)
                with pe.Fori(0, KC) as i:
                    free = ch * ACT_READS + i * 5 + (EC0 + CREDIT)
                    pe.wait_ge(w_ready[0], ch * S0["n"] + i + (S0["C"] + 1 + CREDIT))
                    pe.wait_ge(act_read, free - 4)
                    group(4, TC, 0, 0, KD, h_hi, h_lo, PRE)
                    pe.wait_ge(w_ready[1], ch * S1["n"] + i + (S1["C"] + 1 + CREDIT))
                    tile_with_context(1, 0, free - 3)
                    pe.wait_ge(w_ready[2], ch * S2["n"] + i + (S2["C"] + 1 + CREDIT))
                    tile_with_context(2, 2, free - 1)
                with pe.Fori(0, 2) as i:
                    free = ch * ACT_READS + i * 4 + (EP0 + CREDIT)
                    pe.wait_ge(w_ready[0], ch * S0["n"] + i + (S0["P"] + 1 + CREDIT))
                    tile_with_context(0, 0, free - 3)
                    pe.wait_ge(w_ready[1], ch * S1["n"] + i + (S1["P"] + 1 + CREDIT))
                    tile_with_context(1, 2, free - 1)

                def g1_pass(g):
                    for jj in range(2):
                        free = ch * ACT_READS + g * 4 + (E10 + 2 * jj + CREDIT)
                        read = ch * DVE_READS + g * 4 + (V10 + 2 * jj + CREDIT)
                        pe.wait_ge(w_ready[0], ch * S0["n"] + g * 2 + (S0["G1"] + jj + 1 + CREDIT))
                        pe.wait_ge(act_read, free)
                        group(0, TC, 0, 0, KD, h_hi, h_lo, PRE)
                        pe.wait_ge(w_ready[1], ch * S1["n"] + g * 2 + (S1["G1"] + jj + 1 + CREDIT))
                        pe.wait_ge(act_read, free)
                        group(1, TC, 1, 0, KD, h_hi, h_lo, PRE)
                        pe.wait_ge(w_ready[3], ch * S3["n"] + g * 2 + (S3["G1"] + jj + 1 + CREDIT))
                        pe.wait_ge(d_ready, ch + 1)
                        pe.wait_ge(dve_read, read - 3)
                        group(2 + 2 * jj, TC, 3, 0, 1, d_hi[:, bass.ds(g, 1), :], d_lo[:, bass.ds(g, 1), :])
                        pe.wait_ge(sc_ready, ch * 3 * KC + 3 * KC)
                        pe.wait_ge(dve_read, read - 2)
                        group(3 + 2 * jj, TC, 3, 1, KC, sc_hi, sc_lo)

                g1_pass(0)
                pe.wait_ge(ln_step, ch * LN_STEPS + 2)
                pe.matmul(ps[:, 6, :], mean_of[:, :], u[:, 2, 0:TC], start=True, stop=True).then_inc(stat_done, 1)
                g1_pass(1)
                pe.wait_ge(sum_ready, ch + 1)
                pe.matmul(ps[:, 7, :], mean_of[:, :], u[:, 2, 0:TC], start=True, stop=True).then_inc(stat_done, 1)
                with pe.Fori(2, KC) as g:
                    g1_pass(g)
                with pe.Fori(0, KC) as i:
                    free = ch * ACT_READS + i * 2 + (E20 + CREDIT)
                    read = ch * DVE_READS + i * 2 + (V20 + CREDIT)
                    for jj in range(2):
                        pe.wait_ge(w_ready[jj], ch * S0["n"] + i + (S0["G2"] + 1 + CREDIT))
                        pe.wait_ge(act_read, free - 1 + jj)
                        group(jj, TC, jj, 0, KD, h_hi, h_lo, PRE)
                        uses = S3 if jj else S2
                        pe.wait_ge(w_ready[2 + jj], ch * uses["n"] + i + (uses["G2"] + 1 + CREDIT))
                        pe.wait_ge(ln_step, ch * LN_STEPS + LN_STEPS)
                        pe.wait_ge(dve_read, read - 1 + jj)
                        group(2 + jj, TC, 2 + jj, 0, KC, sa_hi, sa_lo)


NT = T // P
N_GROUPS, PER_GROUP = 4, 8
NE = N_GROUPS * PER_GROUP
TOP_K = 2
BLK = P
COLS = T // BLK
NLOG = N_GROUPS + NE
FAR_BELOW = -3.0e38
N_ROUTE, N_PLACE = 19, 8
R_V, R_E, R_R, R_GM, REC = 8, 10, 12, 14, 16


DE = 256
FT = DE // P


class ExpertWeights:

    def __init__(self, nc, ctx, w1, w3, w2):
        def slots(name, shape):
            return [ctx.enter_context(nc.sbuf_tensor(f"{name}{i}", shape, F32)) for i in range(2)]

        self.w13, self.wd = slots("w13_raw", [P, KD, 2 * DE]), slots("wd_raw", [P, FT, D])
        self.w13_loaded = [[ctx.enter_context(nc.semaphore(f"w13_loaded{i}_{half}")) for half in range(2)] for i in range(2)]
        self.wd_loaded = [ctx.enter_context(nc.semaphore(f"wd_loaded{i}")) for i in range(2)]
        self.views = [w.rearrange("a e (k p) n -> p (a e) k n", p=P) for w in (w1, w3, w2)]

    def load(self, sp, part, slot, e):
        if part == 2:
            sp.dma_start(self.wd[slot][:, :, :], self.views[2][:, bass.ds(e, 1), :, :]).then_inc(self.wd_loaded[slot], 16)
            return
        k = slice(part * KD // 2, (part + 1) * KD // 2)
        for q in range(2):
            sp.dma_start(self.w13[slot][:, k, q * DE:(q + 1) * DE], self.views[q][:, bass.ds(e, 1), k, :]
                         ).then_inc(self.w13_loaded[slot][part], 16)


def project_and_route(nc, ctx, ident, x, merged, w_out, norm_ffn, w_group, b_group, w_router, b_router,
                      x2, hf, table, weights, wo_raw, wo_loaded):
    rec_all = ctx.enter_context(nc.sbuf_tensor("rec_all", [P, NT, REC], F32))
    counts = ctx.enter_context(nc.sbuf_tensor("counts", [P, NE], F32))
    with ExitStack() as inner:
        def sb(name, shape, dt=F32):
            return inner.enter_context(nc.sbuf_tensor(name, shape, dt))

        def sem(name):
            return inner.enter_context(nc.semaphore(name))

        wo_hi, wo_lo = sb("wo_hi", [P, KD, D], F32R), sb("wo_lo", [P, KD, D], F32R)
        m_raw = [sb(f"m_raw{i}", [P, KD, P]) for i in range(4)]
        m_hi = [sb(f"m_hi{i}", [P, KD, P], F32R) for i in range(2)]
        m_lo = [sb(f"m_lo{i}", [P, KD, P], F32R) for i in range(2)]
        xt = [sb(f"xt{i}", [P, D]) for i in range(4)]
        x2t = [sb(f"x2t{i}", [P, D]) for i in range(2)]
        hft = [sb(f"hft{i}", [P, D]) for i in range(2)]
        hft_t = [sb(f"hft_t{i}", [P, KD, P]) for i in range(2)]
        g_ffn = sb("g_ffn", [P, D])
        junk_e = sb("junk_e", [P, 2, NE])
        w_log, b_log = sb("w_log", [P, KD, NLOG]), sb("b_log", [P, NLOG])
        no_one = sb("no_one", [P, NE * COLS], I32)
        iota_e = sb("iota_e", [P, NE])
        iota_i, iota_g = sb("iota_i", [P, NE], I32), sb("iota_g", [P, N_GROUPS])
        before, ones = sb("before", [P, P]), sb("ones", [P, P])
        ms = sb("ms_ffn", [P, 2])
        rec = sb("record", [P, REC])
        le32, oh_g, le = sb("le32", [P, NE]), sb("oh_g", [P, N_GROUPS]), sb("le", [P, 8])
        prod = sb("prod", [P, PER_GROUP, N_GROUPS])
        gm8, gi8, v8, i8 = sb("gm8", [P, 8]), sb("gi8", [P, 8], U32), sb("v8", [P, 8]), sb("i8", [P, 8], U32)
        gif, i2f = sb("gif", [P, 2]), sb("i2f", [P, 2])
        sel, msum = sb("sel", [P, 3, NE]), sb("msum", [P, 2, NE])
        r_i, a_i, c_i = [sb(n, [P, 2], I32) for n in ("r_i", "a_i", "c_i")]
        e_f = sb("e_f", [P, 2])
        place = [sb(f"place{i}", [P, 2], I32) for i in range(2)]
        assigned = [sb(f"assigned{i}", [P, TOP_K], I32) for i in range(2)]
        ps = inner.enter_context(nc.psum_tensor("ps_out", [P, 8, 512], F32))

        m_loaded = [sem(f"m_loaded{i}") for i in range(4)]
        x_loaded = [sem(f"x_loaded{i}") for i in range(4)]
        x2_stored, hf_stored, scattered = ([sem(f"{n}{i}") for i in range(2)] for n in ("x2_stored", "hf_stored", "scattered"))
        wo_hi_done, wo_split, consts, gains, made, m_hi_done, m_lo_done, half_done, x2_done = map(sem, (
            "wo_hi_done", "wo_split", "consts", "gains", "made", "m_hi_done", "m_lo_done", "half_done", "x2_done"))
        ms_step, hf_done, turned, turn_read, logits_done, route_step, rank_done, place_ready = map(sem, (
            "ms_step", "hf_done", "turned", "turn_read", "logits_done", "route_step", "rank_done", "place_ready"))
        place_step, rec_kept, counted = map(sem, ("place_step", "rec_kept", "counted"))
        pool_waited, dve_waited = sem("pool_waited"), sem("dve_waited")
        block = inner.enter_context(nc.Block())
        x_v = x.rearrange("b (t p) n -> p (b t) n", p=P)
        merged_v = merged.rearrange("j p t -> p j t")
        x2_v = x2.rearrange("(t p) n -> p t n", p=P)
        hf_v = hf.rearrange("(t p) n -> p t n", p=P)
        wo_v = w_out.rearrange("a (k p) n -> p (a k) n", p=P)

        def steps(eng, step, rounds=3):
            step(0, 0)
            step(0, 1)
            step(0, 2)
            with eng.Fori(0, rounds) as g:
                for s in (3, 4, 5, 6):
                    step(g, s)
            for g in range(rounds, 3):
                for s in (3, 4, 5, 6):
                    step(g, s)
            step(3, 3)

        @block.sync
        def _(sp):
            def load(g, s):
                i = s % 4
                if s >= 4:
                    sp.wait_ge(m_lo_done, g * 4 + (s - 3))
                    sp.wait_ge(x2_done, g * 4 + (s - 3))
                sp.dma_start(m_raw[i][:, :, :], merged_v[:, :, bass.ds(g * 4 * P + s * P, P)]).then_inc(m_loaded[i], 16)
                sp.dma_start(xt[i][:, :], x_v[:, bass.ds(g * 4 + s, 1), :]).then_inc(x_loaded[i], 16)

            def store(g, s):
                i = s % 2
                sp.wait_ge(x2_done, g * 4 + (s + 1))
                sp.dma_start(x2_v[:, bass.ds(g * 4 + s, 1), :], x2t[i][:, :]).then_inc(x2_stored[i], 16)
                sp.wait_ge(hf_done, g * 4 + (s + 1))
                sp.dma_start(hf_v[:, bass.ds(g * 4 + s, 1), :], hft[i][:, :]).then_inc(hf_stored[i], 16)

            def step(g, s):
                if s >= 1:
                    store(g, s - 1)
                if not (isinstance(g, int) and g * 4 + s + 2 >= NT):
                    load(g, s + 2)
                if isinstance(g, int) and g == 2 and s < 6:
                    for e in range(2):
                        weights.load(sp, s - 3, e, e)

            for s in (*x2_stored, *hf_stored):
                sp.sem_inc(s, CREDIT)
            load(0, 0)
            for k in range(2, KD):
                sp.wait_ge(wo_split, k - 1)
                sp.dma_start(wo_raw[:, k % 2, :], wo_v[:, k, :]).then_inc(wo_loaded[k % 2], 16)
            load(0, 1)
            steps(sp, step, rounds=2)
            store(3, 3)
            for s in (*x2_stored, *hf_stored):
                sp.wait_ge(s, NT // 2 * 16 + CREDIT)

        @block.gpsimd
        def _(pool):
            def split(g, s):
                pool.wait_ge(m_hi_done, g * 4 + (s + 1))
                pool.tensor_tensor(m_lo[s % 2][:, :, :], m_raw[s % 4][:, :, :], m_hi[s % 2][:, :, :].bitcast(F32),
                                   ALU.subtract).then_inc(m_lo_done, 1)

            def scatter(g, s):
                i = s % 2
                pool.wait_ge(place_ready, g * 4 + (s + 1))
                pool.sem_inc(pool_waited, 1)
                for k in range(TOP_K):
                    pool.indirect_dma_start(out=table.rearrange("p (n a) -> (p n) a", a=1),
                                            out_offset=bass.IndirectOffsetOnAxis(ap=place[i][:, k:k + 1], axis=0),
                                            in_=assigned[i][:, k:k + 1], in_offset=None).then_inc(scattered[i], 16)

            def step(g, s):
                if not (isinstance(g, int) and g * 4 + s + 1 >= NT):
                    split(g, s + 1)
                if s >= 3:
                    scatter(g, s - 3)

            split(0, 0)
            pool.iota(no_one[:, :], [[0, NE * COLS]], base=TOP_K * T, channel_multiplier=1).then_inc(made, 1)
            pool.iota(iota_i[:, :], [[1, NE]], base=0, channel_multiplier=0)
            for i in range(2):
                pool.iota(assigned[i][:, :], [[1, TOP_K]], base=(i - 2) * TOP_K * P, channel_multiplier=TOP_K)
            pool.memset(ones[:, :], 1.0)
            pool.memset(msum[:, :, :], 0.0)
            pool.memset(rec[:, :], FAR_BELOW).then_inc(made, 1)
            pool.wait_ge(made, 2)
            pool.affine_select(out=before[:, :], in_=ones[:, :], compare_op=ALU.is_gt, fill=0.0, base=0,
                               pattern=[[1, P]], channel_multiplier=-1).then_inc(made, 1)
            for i in range(4):
                rows = slice(i * P // 4, (i + 1) * P // 4)
                pool.dma_start(table[rows, :], no_one[rows, :]).then_inc(scattered[i % 2], 16)

            for s in scattered:
                pool.wait_ge(s, 32)
            steps(pool, step)
            for s in (1, 2, 3):
                scatter(3, s)
            for s in scattered:
                pool.wait_ge(s, (NT // 2 + 1) * TOP_K * 16)

        @block.scalar
        def _(act):
            def split(g, s):
                act.wait_ge(m_loaded[s % 4], g * 16 + (s // 4 + 1) * 16)
                if s >= 2:
                    act.wait_ge(half_done, g * 8 + 2 * (s - 1))
                act.copy(m_hi[s % 2][:, :, :], m_raw[s % 4][:, :, :]).then_inc(m_hi_done, 1)

            def squares(g, s):
                act.wait_ge(x2_done, g * 4 + (s + 1))
                act.activation(wo_raw[:, 0, :], x2t[s % 2][:, :], ACT.Square, accum_out=ms[:, 0:1]).then_inc(ms_step, 1)

            def root(g, s):
                act.wait_ge(ms_step, g * 16 + (4 * s + 2))
                act.activation(ms[:, 0:1], ms[:, 0:1], ACT.Sqrt).then_inc(ms_step, 1)

            def read_turned(g, s):
                for q in range(2):
                    act.wait_ge(turned, g * 8 + (2 * s + q + 1))
                    act.copy(hft_t[s % 2][:, 4 * q:4 * q + 4, :],
                             ps[:, 4 + q, :].rearrange("p (k n) -> p k n", n=P)).then_inc(turn_read, 1)

            def step(g, s):
                if s >= 1:
                    squares(g, s - 1)
                if not (isinstance(g, int) and g * 4 + s + 1 >= NT):
                    split(g, s + 1)
                if s >= 1:
                    root(g, s - 1)
                    read_turned(g, s - 1)

            for k in range(KD):
                act.wait_ge(wo_loaded[k % 2], (k // 2 + 1) * 16)
                act.copy(wo_hi[:, k, :], wo_raw[:, k % 2, :]).then_inc(wo_hi_done, 1)
                if k == 1:
                    split(0, 0)
            act.dma_start(w_log[:, :, 0:N_GROUPS], w_group.rearrange("a (k p) n -> p (a k) n", p=P)).then_inc(consts, 16)
            act.dma_start(w_log[:, :, N_GROUPS:NLOG], w_router.rearrange("a (k p) n -> p (a k) n", p=P)).then_inc(consts, 16)
            act.dma_start(b_log[:, 0:N_GROUPS], b_group.to_broadcast([P, N_GROUPS])).then_inc(consts, 16)
            act.dma_start(b_log[:, N_GROUPS:NLOG], b_router.to_broadcast([P, NE])).then_inc(consts, 16)
            act.dma_start(g_ffn[:, :], norm_ffn.to_broadcast([P, D])).then_inc(gains, 16)
            steps(act, step)
            squares(3, 3)
            root(3, 3)
            read_turned(3, 3)

        @block.vector
        def _(dve):
            def add(g, s):
                i = s % 2
                dve.wait_ge(half_done, g * 8 + 2 * (s + 1))
                dve.wait_ge(x_loaded[s % 4], g * 16 + (s // 4 + 1) * 16)
                dve.wait_ge(x2_stored[i], g * 32 + ((s // 2) * 16 + CREDIT))
                dve.tensor_tensor(x2t[i][:, :].rearrange("p (a n) -> p a n", a=2), ps[:, 2 * i:2 * i + 2, :],
                                  xt[s % 4][:, :].rearrange("p (a n) -> p a n", a=2), ALU.add).then_inc(x2_done, 1)

            def norm(g, s):
                i = s % 2
                dve.wait_ge(ms_step, g * 16 + (4 * s + 1))
                dve.tensor_scalar(ms[:, 0:1], ms[:, 0:1], 1.0 / D, EPS, ALU.mult, ALU.add).then_inc(ms_step, 1)
                dve.wait_ge(ms_step, g * 16 + (4 * s + 3))
                dve.reciprocal(ms[:, 1:2], ms[:, 0:1]).then_inc(ms_step, 1)
                dve.wait_ge(ms_step, g * 16 + (4 * s + 4))
                dve.wait_ge(hf_stored[i], g * 32 + ((s // 2) * 16 + CREDIT))
                dve.scalar_tensor_tensor(out=hft[i][:, :], in0=x2t[i][:, :], scalar=ms[:, 1:2], in1=g_ffn[:, :],
                                         op0=ALU.mult, op1=ALU.mult).then_inc(hf_done, 1)

            def choose(g, s):
                base = g * 4 * N_ROUTE + s * N_ROUTE
                n = [0]

                def step(ins, wait=True, hold=False):
                    ins.then_inc(route_step, 1)
                    n[0] += 1
                    if wait:
                        dve.wait_ge(route_step, base + n[0])
                    if hold:
                        dve.sem_inc(dve_waited, 1)

                dve.wait_ge(logits_done, g * 4 + (s + 1))
                step(dve.tensor_tensor(rec[:, 0:N_GROUPS], ps[:, 6, 0:N_GROUPS], b_log[:, 0:N_GROUPS], ALU.add), False)
                step(dve.tensor_tensor(le32[:, :], ps[:, 6, N_GROUPS:NLOG], b_log[:, N_GROUPS:NLOG], ALU.add), hold=True)
                step(dve.max(gm8[:, :], rec[:, 0:8]), hold=True)
                step(dve.max_index(gi8[:, :], gm8[:, :], rec[:, 0:8]))
                step(dve.tensor_copy(gif[:, 0:1], gi8[:, 0:1]))
                step(dve.tensor_scalar(oh_g[:, :], iota_g[:, :], gif[:, 0:1], None, ALU.is_equal), False)
                step(dve.tensor_scalar(gif[:, 1:2], gif[:, 0:1], float(PER_GROUP), None, ALU.mult))
                step(dve.tensor_tensor(prod[:, :, :], le32[:, :].rearrange("p (g e) -> p e g", g=N_GROUPS),
                                       oh_g[:, :].unsqueeze(1).to_broadcast([P, PER_GROUP, N_GROUPS]), ALU.mult))
                step(dve.tensor_reduce(le[:, :], prod[:, :, :], mybir.AxisListType.X, ALU.add), hold=True)
                step(dve.max(v8[:, :], le[:, :]), hold=True)
                step(dve.max_index(i8[:, :], v8[:, :], le[:, :]))
                step(dve.tensor_copy(i2f[:, :], i8[:, 0:2]))
                step(dve.tensor_scalar(rec[:, R_E:R_E + 2], i2f[:, :], gif[:, 1:2], None, ALU.add))
                for k in range(TOP_K):
                    step(dve.tensor_scalar(sel[:, k, :], iota_e[:, :], rec[:, R_E + k:R_E + k + 1], None, ALU.is_equal), k == 1)
                step(dve.tensor_tensor(sel[:, 2, :], sel[:, 0, :], sel[:, 1, :], ALU.add))
                step(dve.tensor_tensor(msum[:, (s + 1) % 2, :], msum[:, s % 2, :], sel[:, 2, :], ALU.add), False)
                step(dve.tensor_copy(rec[:, R_V:R_V + 2], v8[:, 0:2]), False)
                assert n[0] == N_ROUTE - 1
                dve.tensor_copy(rec[:, R_GM:R_GM + 1], gm8[:, 0:1]).then_inc(route_step, 1)

            def place_tokens(g, s):
                i = s % 2
                base = g * 4 * N_PLACE + s * N_PLACE
                dve.wait_ge(route_step, g * 4 * N_ROUTE + (s + 1) * N_ROUTE)
                dve.wait_ge(rank_done, g * 4 + (s + 1))
                for k in range(TOP_K):
                    dve.tensor_tensor(junk_e[:, k, :], sel[:, k, :], ps[:, 7, 0:NE], ALU.mult).then_inc(place_step, 1)
                dve.wait_ge(place_step, base + 2)
                dve.tensor_reduce(rec[:, R_R:R_R + 2], junk_e[:, :, :], mybir.AxisListType.X, ALU.add).then_inc(place_step, 1)
                dve.wait_ge(place_step, base + 3)
                dve.tensor_copy(r_i[:, :], rec[:, R_R:R_R + 2]).then_inc(place_step, 1)
                dve.tensor_scalar(e_f[:, :], rec[:, R_E:R_E + 2], float(COLS), None, ALU.mult).then_inc(place_step, 1)
                dve.tensor_copy(rec_all[:, bass.ds(g * 4 + s, 1), :], rec[:, :]).then_inc(rec_kept, 1)
                dve.wait_ge(place_step, base + 5)
                dve.tensor_scalar(a_i[:, :], r_i[:, :], BLK - 1, (NE * COLS).bit_length() - 1, ALU.bitwise_and,
                                  ALU.logical_shift_left).then_inc(place_step, 1)
                dve.tensor_scalar(c_i[:, :], r_i[:, :], BLK.bit_length() - 1, None, ALU.logical_shift_right).then_inc(place_step, 1)
                dve.wait_ge(place_step, base + 7)
                dve.scalar_tensor_tensor(out=e_f[:, :], in0=c_i[:, :], scalar=1.0, in1=e_f[:, :], op0=ALU.mult,
                                         op1=ALU.add).then_inc(place_step, 1)
                dve.wait_ge(scattered[i], g * 64 + ((s // 2) * 32 + 32))
                dve.tensor_scalar(assigned[i][:, :], assigned[i][:, :], 2.0 * TOP_K * P, None, ALU.add)
                dve.wait_ge(place_step, base + 8)
                dve.scalar_tensor_tensor(out=place[i][:, :], in0=a_i[:, :], scalar=1.0, in1=e_f[:, :], op0=ALU.mult,
                                         op1=ALU.add).then_inc(place_ready, 1)
                dve.wait_ge(rec_kept, g * 4 + (s + 1))

            def step(g, s):
                if s >= 1:
                    add(g, s - 1)
                if s >= 3:
                    place_tokens(g, s - 3)
                if s >= 1:
                    norm(g, s - 1)
                if s >= 2:
                    choose(g, s - 2)

            for k in range(KD):
                dve.wait_ge(wo_hi_done, k + 1)
                dve.tensor_tensor(wo_lo[:, k, :], wo_raw[:, k % 2, :], wo_hi[:, k, :].bitcast(F32),
                                  ALU.subtract).then_inc(wo_split, 1)
            dve.wait_ge(made, 3)
            dve.tensor_copy(iota_e[:, :], iota_i[:, :])
            dve.tensor_copy(iota_g[:, :], iota_i[:, 0:N_GROUPS]).then_inc(made, 1)
            dve.wait_ge(made, 4)
            dve.wait_ge(gains, 16)
            dve.wait_ge(consts, 64)
            steps(dve, step)
            add(3, 3)
            place_tokens(3, 1)
            norm(3, 3)
            choose(3, 2)
            place_tokens(3, 2)
            choose(3, 3)
            place_tokens(3, 3)
            dve.wait_ge(counted, 1)
            dve.tensor_copy(counts[:, :], ps[:, 7, 0:NE]).then_inc(counted, 1)
            dve.wait_ge(counted, 2)

        @block.tensor
        def _(pe):
            def start_tile(g, s):
                pe.wait_ge(m_lo_done, g * 4 + (s + 1))
                if s >= 2:
                    pe.wait_ge(x2_done, g * 4 + (s - 1))

            def part(s, q, ks):
                i, n = s % 2, slice(q * 512, (q + 1) * 512)
                for k in ks:
                    last = three_products(pe, ps[:, 2 * i + q, :], m_hi[i][:, k, :], m_lo[i][:, k, :],
                                          wo_hi[:, k, n], wo_lo[:, k, n], k == 0, k == KD - 1)
                if k == KD - 1:
                    last.then_inc(half_done, 1)

            def turn(g, s):
                pe.wait_ge(hf_done, g * 4 + (s + 1))
                for q in range(2):
                    if s >= 1:
                        pe.wait_ge(turn_read, g * 8 + (2 * (s - 1) + q + 1))
                    for k in range(4):
                        last = pe.transpose(ps[:, 4 + q, k * P:(k + 1) * P], hft[s % 2][:, (4 * q + k) * P:(4 * q + k + 1) * P],
                                            ident[:, :])
                    last.then_inc(turned, 1)

            def logits(g, s):
                pe.wait_ge(turn_read, g * 8 + 2 * (s + 1))
                if s >= 1:
                    pe.wait_ge(route_step, g * 4 * N_ROUTE + ((s - 1) * N_ROUTE + 2))
                for k in range(KD):
                    last = pe.matmul(ps[:, 6, 0:NLOG], hft_t[s % 2][:, k, :], w_log[:, k, :], start=k == 0, stop=k == KD - 1)
                last.then_inc(logits_done, 1)

            def ranks(g, s):
                pe.wait_ge(route_step, g * 4 * N_ROUTE + (s + 1) * N_ROUTE)
                pe.matmul(ps[:, 7, 0:NE], before[:, :], sel[:, 2, :], start=True, stop=False)
                pe.matmul(ps[:, 7, 0:NE], ones[:, :], msum[:, s % 2, :], start=False, stop=True).then_inc(rank_done, 1)

            def step(g, s):
                start_tile(g, s)
                if s == 0:
                    for k in range(KD):
                        pe.wait_ge(wo_split, k + 1)
                        part(0, 0, [k])
                        part(0, 1, [k])
                    return
                part(s, 0, range(0, KD // 2))
                if s == 1:
                    pe.wait_ge(made, 4)
                    pe.wait_ge(consts, 64)
                if s >= 3:
                    ranks(g, s - 3)
                part(s, 0, range(KD // 2, KD))
                part(s, 1, range(0, KD // 2))
                turn(g, s - 1)
                part(s, 1, range(KD // 2, KD))
                logits(g, s - 1)

            steps(pe, step)
            ranks(3, 1)
            turn(3, 3)
            logits(3, 3)
            ranks(3, 2)
            ranks(3, 3)
            pe.wait_ge(place_ready, NT)
            pe.matmul(ps[:, 7, 0:NE], ones[:, :], msum[:, NT % 2, :], start=True, stop=True).then_inc(counted, 1)
    return rec_all, counts


SPLIT_13 = 4
DEEP = 4
AHEAD = DEEP
BEHIND = 4
STEP_13 = KD // SPLIT_13
N_PLAN = 7
MAX_BLOCKS = T * TOP_K // BLK + NE


def experts(nc, ctx, ident, rec_all, counts, hf, table, weights, y, x2, x2_ahead, x2_ahead_loaded):
    y_weight = ctx.enter_context(nc.sbuf_tensor("y_weight", [P, NT, TOP_K], F32))
    w13_raw, wd_raw, w13_loaded, wd_loaded = weights.w13, weights.wd, weights.w13_loaded, weights.wd_loaded
    with ExitStack() as inner:
        def sb(name, shape, dt=F32):
            return inner.enter_context(nc.sbuf_tensor(name, shape, dt))

        def sem(name):
            return inner.enter_context(nc.semaphore(name))

        w13_hi, w13_lo = ([sb(f"w13_{h}{i}", [P, KD, 2 * DE], F32R) for i in range(2)] for h in ("hi", "lo"))
        wd_hi, wd_lo = ([sb(f"wd_{h}{i}", [P, FT, D], F32R) for i in range(2)] for h in ("hi", "lo"))
        index = sb("index", [P, NE * COLS], I32)
        token = sb("token", [P, NE * COLS], I32)
        now = sb("now", [P, 1], I32)
        recent, newest = sb("recent", [P, BEHIND + 1], I32), sb("newest", [P, BEHIND], I32)
        place = [sb(f"y_place{i}", [P, 1], I32) for i in range(2)]
        xg = sb("xg", [P, 2, D])
        x_hi, x_lo = (sb(f"xg_{h}", [P, KD, P], F32R) for h in ("hi", "lo"))
        warm = sb("warm", [P, 2])
        sig, hid = sb("sig", [P, DE]), sb("hid", [P, DE])
        hid_hi, hid_lo = (sb(f"hid_{h}", [P, FT, P], F32R) for h in ("hi", "lo"))
        y_sb = sb("y_sb", [P, 2, D])
        more = sb("more", [P, NE], I32)
        first = sb("first", [P, NE + 2], I32)
        nb_i, nb, ones_e = sb("nb_i", [P, NE], I32), sb("nb", [P, NE]), sb("ones_e", [P, NE])
        first_f = sb("first_f", [P, NE + 1])
        ex, ex_v = sb("ex", [P, NT, N_GROUPS]), sb("ex_v", [P, NT])
        tot = sb("tot", [P, NT])
        ps = inner.enter_context(nc.psum_tensor("ps_moe", [P, 8, 512], F32))

        w13_hi_done, w13_split, wd_hi_done, wd_split = (
            [sem(f"{n}{i}") for i in range(2)] for n in ("w13_hi_done", "w13_split", "wd_hi_done", "wd_split"))
        plan, index_loaded, token_set, now_set, shifted, gathered, x_ready, turned, x_hi_done, x_read = map(sem, (
            "plan", "index_loaded", "token_set", "now_set", "shifted", "gathered", "x_ready", "rows_turned", "x_hi_done", "x_read"))
        up_done, sig_done, hid_step, hid_ready, hid_turned, hid_hi_done, hid_read = map(sem, (
            "up_done", "sig_done", "hid_step", "hid_ready", "hid_turned", "hid_hi_done", "hid_read"))
        down_done, y_read_act, y_read_dve, place_set, y_stored, y_free = map(sem, (
            "down_done", "y_read_act", "y_read_dve", "place_set", "y_stored", "y_free"))
        weigh, weigh_act, cleared, pool_waited = map(sem, ("weigh", "weigh_act", "cleared", "pool_waited2"))
        block = inner.enter_context(nc.Block())
        x2_v = x2.rearrange("(t p) n -> p t n", p=P)

        def blocks(eng, body):
            def experts_of(pair):
                for p in range(2):
                    b0 = eng.value_load(first[0:1, bass.ds(pair * 2 + (p + 1), 1)], min_val=0, max_val=MAX_BLOCKS)
                    n = eng.value_load(more[0:1, bass.ds(pair * 2 + p, 1)], min_val=0, max_val=COLS - 1)
                    body(b0, p, pair, True)
                    with eng.If(n > 0):
                        with eng.Fori(0, n) as c:
                            body(b0 + c + 1, p, pair, False)

            with eng.Fori(0, NE // 2 - 1) as pair:
                experts_of(pair)
            experts_of(NE // 2 - 1)

        def for_next(split, p, pair, *parts):
            if p == 0:
                split(1, pair, *parts)
            elif not isinstance(pair, int):
                split(0, pair + 1, *parts)

        @block.sync
        def _(sp):
            sp.dma_start(index[:, :], table).then_inc(index_loaded, 16)

            with sp.Fori(1, NE // 2) as pair:
                for p in range(2):
                    for half in range(2):
                        sp.wait_ge(w13_split[p], pair * SPLIT_13 + (half - 1) * (SPLIT_13 // 2))
                        weights.load(sp, half, p, pair * 2 + p)
                    sp.wait_ge(wd_split[p], pair * FT + (p * FT))
                    weights.load(sp, 2, p, pair * 2 + p)
            for t in range(0, AHEAD, 2):
                sp.dma_start(x2_ahead[:, t:t + 2, :], x2_v[:, t:t + 2, :]).then_inc(x2_ahead_loaded, 16)

        @block.gpsimd
        def _(pool):
            def remember(col, b):
                pool.tensor_copy(newest[:, :], recent[:, 0:BEHIND]).then_inc(shifted, 1)
                pool.wait_ge(shifted, b * 3 + 1)
                pool.sem_inc(pool_waited, 1)
                pool.tensor_copy(recent[:, 1:BEHIND + 1], newest[:, :]).then_inc(shifted, 1)
                pool.tensor_copy(recent[:, 0:1], index[:, bass.ds(col, 1)]).then_inc(shifted, 1)
                pool.tensor_copy(now[:, :], token[:, bass.ds(col, 1)]).then_inc(now_set, 1)

            def gather(b, i):
                pool.wait_ge(turned, b + (CREDIT - 1))
                pool.wait_ge(now_set, b + 1)
                pool.sem_inc(pool_waited, 1)
                pool.indirect_dma_start(out=xg[:, i, :], out_offset=None, in_=hf,
                                        in_offset=bass.IndirectOffsetOnAxis(ap=now[:, 0:1], axis=0),
                                        bounds_check=T - 1, oob_is_err=False).then_inc(gathered, 16)

            def scatter(b, i):
                pool.wait_ge(shifted, b * 3 + 3)
                pool.sem_inc(pool_waited, 1)
                pool.tensor_copy(place[i][:, :], recent[:, BEHIND:BEHIND + 1]).then_inc(place_set, 1)
                pool.wait_ge(y_stored, b * 16 + 16)
                pool.sem_inc(y_free, 1)
                pool.wait_ge(y_read_act, b + (CREDIT - 2))
                pool.wait_ge(y_read_dve, b + (CREDIT - 2))
                pool.wait_ge(place_set, b + 2)
                pool.sem_inc(pool_waited, 1)
                put_away(i)

            def put_away(i):
                pool.indirect_dma_start(out=y, out_offset=bass.IndirectOffsetOnAxis(ap=place[i][:, 0:1], axis=0),
                                        in_=y_sb[:, i, :], in_offset=None, bounds_check=TOP_K * T - 1,
                                        oob_is_err=False).then_inc(y_stored, 16)

            def step(col, b, loads):
                remember(col, b)
                for i in range(2):
                    with pool.If((b & 1) == i):
                        if loads:
                            gather(b, i)
                        scatter(b, i)
                if loads:
                    pool.wait_ge(gathered, b * 16 + 16)
                    pool.sem_inc(x_ready, 1)

            pool.memset(y_sb[:, :, :], 0.0)
            pool.iota(recent[:, :], [[0, BEHIND + 1]], base=TOP_K * T, channel_multiplier=1)
            pool.iota(place[1][:, :], [[0, 1]], base=TOP_K * T, channel_multiplier=1).then_inc(place_set, 1)
            pool.memset(warm[:, :], 0.0)
            pool.memset(hid[:, :], 0.0).then_inc(cleared, 1)
            pool.wait_ge(cleared, 1)
            pool.wait_ge(place_set, 1)
            put_away(1)
            pool.wait_ge(index_loaded, 16)
            pool.wait_ge(token_set, 2)
            pool.wait_ge(plan, N_PLAN)
            with pool.Fori(0, NE) as e:
                b0 = pool.value_load(first[0:1, bass.ds(e + 1, 1)], min_val=0, max_val=MAX_BLOCKS)
                n = pool.value_load(more[0:1, bass.ds(e, 1)], min_val=0, max_val=COLS - 1)
                with pool.Fori(0, n + 1) as c:
                    step(e * COLS + c, b0 + c, True)
            last = pool.value_load(first[0:1, NE + 1:NE + 2], min_val=0, max_val=MAX_BLOCKS)
            step(0, last, True)
            for more_steps in range(1, BEHIND):
                step(0, last + more_steps, False)
            pool.wait_ge(y_stored, last * 16 + (BEHIND + 1) * 16)
            pool.sem_inc(pool_waited, 1)

        @block.scalar
        def _(act):
            def split_13(p, n):
                for q in range(SPLIT_13):
                    if q % (SPLIT_13 // 2) == 0:
                        act.wait_ge(w13_loaded[p][q // (SPLIT_13 // 2)], n * 32 + 32)
                    k = slice(q * STEP_13, (q + 1) * STEP_13)
                    act.copy(w13_hi[p][:, k, :], w13_raw[p][:, k, :]).then_inc(w13_hi_done[p], 1)

            def split_d(p, n):
                act.wait_ge(wd_loaded[p], n * 16 + 16)
                for k in range(FT):
                    act.copy(wd_hi[p][:, k, :], wd_raw[p][:, k, :]).then_inc(wd_hi_done[p], 1)

            def x_high(b):
                act.wait_ge(turned, b + (1 + CREDIT))
                act.copy(x_hi[:, :, :].rearrange("p (a k) n -> p a (k n)", a=2), ps[:, 0:2, :]).then_inc(x_hi_done, 1)

            def read_y(b):
                act.wait_ge(down_done, b + (1 + CREDIT))
                act.wait_ge(y_free, b + 3)
                act.copy(y_sb[:, bass.ds((b + 1) & 1, 1), 0:512], ps[:, 2, :]).then_inc(y_read_act, 1)

            def body(b, p, pair, new):
                if new:
                    act.activation(warm[:, 1:2], warm[:, 0:1], ACT.Sigmoid)
                    for_next(split_13, p, pair)
                act.wait_ge(up_done, b + (1 + CREDIT))
                act.activation(sig[:, :], ps[:, 4, 0:DE], ACT.Sigmoid).then_inc(sig_done, 1)
                x_high(b + 1)
                read_y(b)
                act.wait_ge(hid_turned, b + 1)
                act.copy(hid_hi[:, :, :].rearrange("p k n -> p (k n)"), ps[:, 5, 0:DE]).then_inc(hid_hi_done, 1)
                if new:
                    for_next(split_d, p, pair)

            act.sem_inc(y_read_act, CREDIT)
            split_13(0, 0)
            act.wait_ge(cleared, 1)
            for k in range(FT):
                act.copy(wd_hi[1][:, k, :], y_sb[:, 0, :])
            act.copy(hid_hi[:, :, :].rearrange("p k n -> p (k n)"), hid[:, :]).then_inc(cleared, 1)
            split_d(0, 0)
            act.wait_ge(weigh, 2)
            act.activation(ex[:, :, :], ex[:, :, :], ACT.Exp).then_inc(weigh_act, 1)
            act.activation(ex_v[:, :], ex_v[:, :], ACT.Exp).then_inc(weigh_act, 1)
            act.wait_ge(plan, N_PLAN)
            x_high(0)
            blocks(act, body)
            last = act.value_load(first[0:1, NE + 1:NE + 2], min_val=0, max_val=MAX_BLOCKS)
            read_y(last)

        @block.vector
        def _(dve):
            def split_13(p, n, parts=range(SPLIT_13)):
                for q in parts:
                    k = slice(q * STEP_13, (q + 1) * STEP_13)
                    dve.wait_ge(w13_hi_done[p], n * SPLIT_13 + (q + 1))
                    dve.tensor_tensor(w13_lo[p][:, k, :], w13_raw[p][:, k, :], w13_hi[p][:, k, :].bitcast(F32),
                                      ALU.subtract).then_inc(w13_split[p], 1)

            def split_d(p, n):
                for k in range(FT):
                    dve.wait_ge(wd_hi_done[p], n * FT + (k + 1))
                    dve.tensor_tensor(wd_lo[p][:, k, :], wd_raw[p][:, k, :], wd_hi[p][:, k, :].bitcast(F32),
                                      ALU.subtract).then_inc(wd_split[p], 1)

            dve.sem_inc(hid_read, CREDIT)
            dve.sem_inc(y_read_dve, CREDIT)
            dve.tensor_scalar(nb_i[:, :], counts[:, :], float(BLK - 1), None, ALU.add).then_inc(plan, 1)
            dve.wait_ge(plan, 1)
            dve.tensor_scalar(nb_i[:, :], nb_i[:, :], BLK.bit_length() - 1, None, ALU.logical_shift_right).then_inc(plan, 1)
            dve.wait_ge(plan, 2)
            dve.tensor_scalar(nb[:, :], nb_i[:, :], 1.0, None, ALU.max).then_inc(plan, 1)
            dve.memset(ones_e[:, :], 1.0)
            dve.memset(first_f[:, 0:1], 0.0)
            dve.memset(first[:, 0:2], 0).then_inc(plan, 1)
            dve.wait_ge(plan, 4)
            dve.tensor_scalar(more[:, :], nb[:, :], -1.0, None, ALU.add).then_inc(plan, 1)
            dve.tensor_tensor_scan(first_f[:, 1:NE + 1], ones_e[:, :], nb[:, :], 0.0, ALU.mult, ALU.add).then_inc(plan, 1)
            dve.wait_ge(plan, 6)
            dve.tensor_copy(first[:, 1:NE + 2], first_f[:, :]).then_inc(plan, 1)
            dve.memset(xg[:, :, :], 0.0).then_inc(token_set, 1)
            dve.wait_ge(index_loaded, 16)
            dve.tensor_scalar(token[:, :], index[:, :], TOP_K.bit_length() - 1, None,
                              ALU.logical_shift_right).then_inc(token_set, 1)
            split_13(0, 0)
            dve.wait_ge(cleared, 1)
            for k in range(FT):
                dve.tensor_copy(wd_lo[1][:, k, :], y_sb[:, 0, :]).then_inc(wd_split[1], 1)
            dve.tensor_copy(hid_lo[:, :, :].rearrange("p k n -> p (k n)"), hid[:, :]).then_inc(cleared, 1)
            split_d(0, 0)
            dve.tensor_tensor(ex[:, :, :], rec_all[:, :, 0:N_GROUPS],
                              rec_all[:, :, R_GM:R_GM + 1].to_broadcast([P, NT, N_GROUPS]), ALU.subtract).then_inc(weigh, 1)
            dve.tensor_tensor(ex_v[:, :], rec_all[:, :, R_V + 1], rec_all[:, :, R_V], ALU.subtract).then_inc(weigh, 1)
            dve.wait_ge(weigh_act, 2)
            dve.tensor_reduce(tot[:, :], ex[:, :, :], mybir.AxisListType.X, ALU.add).then_inc(weigh, 1)
            dve.wait_ge(weigh, 3)
            dve.scalar_tensor_tensor(out=tot[:, :], in0=ex_v[:, :], scalar=1.0, in1=tot[:, :], op0=ALU.add,
                                     op1=ALU.mult).then_inc(weigh, 1)
            dve.wait_ge(weigh, 4)
            dve.reciprocal(y_weight[:, :, 0], tot[:, :]).then_inc(weigh, 1)
            dve.wait_ge(weigh, 5)
            dve.tensor_tensor(y_weight[:, :, 1], y_weight[:, :, 0], ex_v[:, :], ALU.mult).then_inc(weigh, 1)

            def x_low(b):
                dve.wait_ge(x_hi_done, b + 1)
                dve.tensor_tensor(x_lo[:, :, :].rearrange("p (a k) n -> p a (k n)", a=2), ps[:, 0:2, :],
                                  x_hi[:, :, :].rearrange("p (a k) n -> p a (k n)", a=2).bitcast(F32),
                                  ALU.subtract).then_inc(x_read, 1)

            def read_y(b):
                dve.wait_ge(down_done, b + (1 + CREDIT))
                dve.wait_ge(y_free, b + 3)
                dve.tensor_copy(y_sb[:, bass.ds((b + 1) & 1, 1), 512:1024], ps[:, 3, :]).then_inc(y_read_dve, 1)

            def body(b, p, pair, new):
                if new:
                    for_next(split_13, p, pair, range(SPLIT_13 - 1))
                dve.wait_ge(sig_done, b + 1)
                dve.tensor_tensor(sig[:, :], ps[:, 4, 0:DE], sig[:, :], ALU.mult).then_inc(hid_step, 1)
                dve.wait_ge(hid_step, b + 1)
                dve.tensor_tensor(hid[:, :], ps[:, 4, DE:2 * DE], sig[:, :], ALU.mult).then_inc(hid_ready, 1)
                x_low(b + 1)
                if new:
                    for_next(split_13, p, pair, [SPLIT_13 - 1])
                read_y(b)
                dve.wait_ge(hid_hi_done, b + 1)
                dve.tensor_tensor(hid_lo[:, :, :].rearrange("p k n -> p (k n)"), ps[:, 5, 0:DE],
                                  hid_hi[:, :, :].rearrange("p k n -> p (k n)").bitcast(F32), ALU.subtract).then_inc(hid_read, 1)
                if new:
                    for_next(split_d, p, pair)

            x_low(0)
            blocks(dve, body)
            last = dve.value_load(first[0:1, NE + 1:NE + 2], min_val=0, max_val=MAX_BLOCKS)
            read_y(last)

        @block.tensor
        def _(pe):
            def turn_from(i):
                for k in range(KD):
                    last = pe.transpose(ps[:, k // 4, (k % 4) * P:(k % 4 + 1) * P], xg[:, i, k * P:(k + 1) * P], ident[:, :])
                last.then_inc(turned, 1)

            def turn(b):
                pe.wait_ge(x_ready, b + 1)
                for i in range(2):
                    with pe.If((b & 1) == i):
                        turn_from(i)

            def down(b, p):
                pe.wait_ge(hid_read, b + CREDIT)
                pe.wait_ge(y_read_act, b + CREDIT)
                pe.wait_ge(y_read_dve, b + CREDIT)
                for q in range(2):
                    for k in range(FT):
                        n = slice(q * 512, (q + 1) * 512)
                        last = three_products(pe, ps[:, 2 + q, :], hid_hi[:, k, :], hid_lo[:, k, :],
                                              wd_hi[p][:, k, n], wd_lo[p][:, k, n], k == 0, k == FT - 1)
                last.then_inc(down_done, 1)

            def body(b, p, pair, new):
                pe.wait_ge(x_read, b + 1)
                for k in range(KD):
                    if new and k % STEP_13 == 0:
                        pe.wait_ge(w13_split[p], pair * SPLIT_13 + (k // STEP_13 + 1))
                    last = three_products(pe, ps[:, 4, :], x_hi[:, k, :], x_lo[:, k, :],
                                          w13_hi[p][:, k, :], w13_lo[p][:, k, :], k == 0, k == KD - 1)
                last.then_inc(up_done, 1)
                turn(b + 1)
                of = 1 - p if new else p
                pe.wait_ge(wd_split[of], pair * FT + (FT * 2 if p and not new else FT))
                down(b, of)
                pe.wait_ge(hid_ready, b + 1)
                for k in range(FT):
                    last = pe.transpose(ps[:, 5, k * P:(k + 1) * P], hid[:, k * P:(k + 1) * P], ident[:, :])
                last.then_inc(hid_turned, 1)

            for s in (turned, up_done, down_done):
                pe.sem_inc(s, CREDIT)
            pe.wait_ge(cleared, 3)
            pe.wait_ge(plan, N_PLAN)
            pe.wait_ge(x_ready, 1)
            turn_from(0)
            blocks(pe, body)
            last = pe.value_load(first[0:1, NE + 1:NE + 2], min_val=0, max_val=MAX_BLOCKS)
            pe.wait_ge(wd_split[1], (NE // 2 + 1) * FT)
            down(last, 1)
    return y_weight




def combine(nc, y_weight, x2, x2_ahead, x2_ahead_loaded, y, final_norm, out):
    with ExitStack() as inner:
        def sb(name, shape, dt=F32):
            return inner.enter_context(nc.sbuf_tensor(name, shape, dt))

        def sem(name):
            return inner.enter_context(nc.semaphore(name))

        g_out = sb("g_out", [P, D])
        xt = [sb(f"x2_{i}", [P, D]) for i in range(DEEP)]
        yt = [sb(f"y_{i}", [P, TOP_K, D]) for i in range(DEEP)]
        ot = [sb(f"o_{i}", [P, D]) for i in range(DEEP)]
        ms = [sb(f"ms_{i}", [P, 2]) for i in range(DEEP)]
        x_loaded = [sem(f"x2_loaded{i}") for i in range(DEEP)]
        y_loaded = [sem(f"y_loaded{i}") for i in range(DEEP)]
        out_stored = [sem(f"out_stored{i}") for i in range(DEEP)]
        gains, first_added, summed, ms_step, normed, act_waited = map(
            sem, ("gains3", "first_added", "summed", "ms_step3", "normed3", "act_waited3"))
        block = inner.enter_context(nc.Block())
        x2_v = x2.rearrange("(t p) n -> p t n", p=P)
        y_v = y.rearrange("(t p k) n -> p t k n", p=P, k=TOP_K)
        out_v = out.rearrange("b (t p) n -> p (b t) n", p=P)
        rounds, rounds_ahead = NT // DEEP, AHEAD // DEEP

        def tiles(eng, *parts):
            def one_round(g, xs, here):
                for i in range(DEEP + len(parts) - 1):
                    for late, part in enumerate(parts):
                        if 0 <= i - late < DEEP:
                            part(g, i - late, xs[i - late], here)

            with eng.Fori(0, rounds_ahead) as g:
                one_round(g, [x2_ahead[:, bass.ds(g * DEEP + i, 1), :].rearrange("p o n -> p (o n)")
                              for i in range(DEEP)], True)
            with eng.Fori(rounds_ahead, rounds) as g:
                one_round(g, [x[:, :] for x in xt], False)

        @block.sync
        def _(sp):
            def load(g, i, x, here):
                n = g * DEEP + i
                sp.wait_ge(normed, n + (1 - DEEP + CREDIT))
                sp.dma_start(yt[i][:, :, :], y_v[:, bass.ds(n, 1), :, :]).then_inc(y_loaded[i], 16)
                if not here:
                    sp.dma_start(x, x2_v[:, bass.ds(n, 1), :]).then_inc(x_loaded[i], 16)

            sp.dma_start(g_out[:, :], final_norm.unsqueeze(0).to_broadcast([P, D])).then_inc(gains, 16)
            sp.sem_inc(normed, CREDIT)
            for s in x_loaded:
                sp.sem_inc(s, rounds_ahead * 16)
            tiles(sp, load)

        @block.scalar
        def _(act):
            def root_mean_square(g, i, x, here):
                n = g * DEEP + i
                act.wait_ge(summed, n + 1)
                act.wait_ge(out_stored[i], g * 16 + CREDIT)
                act.activation(ot[i][:, :], x, ACT.Square, accum_out=ms[i][:, 0:1]).then_inc(ms_step, 1)
                act.wait_ge(ms_step, n * 4 + 2)
                act.activation(ms[i][:, 0:1], ms[i][:, 0:1], ACT.Sqrt).then_inc(ms_step, 1)
                act.wait_ge(normed, n + (1 + CREDIT))
                act.sem_inc(act_waited, 1)
                act.dma_start(out_v[:, bass.ds(n, 1), :], ot[i][:, :]).then_inc(out_stored[i], 16)

            for s in out_stored:
                act.sem_inc(s, CREDIT)
            tiles(act, root_mean_square)
            for s in out_stored:
                act.wait_ge(s, rounds * 16 + CREDIT)

        @block.vector
        def _(dve):
            def add(g, i, x, here):
                n = g * DEEP + i
                if not here:
                    dve.wait_ge(x_loaded[i], g * 16 + 16)
                dve.wait_ge(y_loaded[i], g * 16 + 16)
                dve.scalar_tensor_tensor(out=x, in0=yt[i][:, 0, :], scalar=y_weight[:, bass.ds(n, 1), 0],
                                         in1=x, op0=ALU.mult, op1=ALU.add).then_inc(first_added, 1)
                dve.wait_ge(first_added, n + 1)
                dve.scalar_tensor_tensor(out=x, in0=yt[i][:, 1, :], scalar=y_weight[:, bass.ds(n, 1), 1],
                                         in1=x, op0=ALU.mult, op1=ALU.add).then_inc(summed, 1)

            def norm(g, i, x, here):
                n = g * DEEP + i
                dve.wait_ge(ms_step, n * 4 + 1)
                dve.tensor_scalar(ms[i][:, 0:1], ms[i][:, 0:1], 1.0 / D, EPS, ALU.mult, ALU.add).then_inc(ms_step, 1)
                dve.wait_ge(ms_step, n * 4 + 3)
                dve.reciprocal(ms[i][:, 1:2], ms[i][:, 0:1]).then_inc(ms_step, 1)
                dve.wait_ge(ms_step, n * 4 + 4)
                dve.scalar_tensor_tensor(out=ot[i][:, :], in0=x, scalar=ms[i][:, 1:2], in1=g_out[:, :],
                                         op0=ALU.mult, op1=ALU.mult).then_inc(normed, 1)

            dve.wait_ge(gains, 16)
            dve.wait_ge(x2_ahead_loaded, AHEAD // 2 * 16)
            tiles(dve, add, norm)


def build(nc, x, meta, norm_mix, w_in, conv_w, conv_b, conv_ln_g, conv_ln_b, w_conv_out, pool_w, pool_scale, sc_w,
          w_sc_out, w_out, norm_ffn, w_group, b_group, w_router, b_router, w1, w3, w2, final_norm, out):
    merged = nc.dram_tensor("merged", (KD, P, T), F32).ap()
    x2 = nc.dram_tensor("x2", (T, D), F32).ap()
    hf = nc.dram_tensor("hf", (T, D), F32).ap()
    table = nc.dram_tensor("table", (P, NE * COLS), I32).ap()
    y = nc.dram_tensor("y", (TOP_K * T, D), F32).ap()
    with ExitStack() as kept:
        ident = kept.enter_context(nc.sbuf_tensor("ident", [P, P], F32))
        wo_raw = kept.enter_context(nc.sbuf_tensor("wo_raw", [P, 2, D], F32))
        wo_loaded = [kept.enter_context(nc.semaphore(f"wo_loaded{i}")) for i in range(2)]
        with ExitStack() as stage:
            c = setup(nc, stage, ident, x, meta, w_in, pool_w, w_sc_out, norm_mix, conv_w, conv_b, conv_ln_g,
                      conv_ln_b, pool_scale, sc_w, w_out, wo_raw, wo_loaded)
            mixer(nc, c, x, w_in, w_conv_out, pool_w, w_sc_out, merged)
        weights = ExpertWeights(nc, kept, w1, w3, w2)
        rec_all, counts = project_and_route(nc, kept, ident, x, merged, w_out, norm_ffn, w_group, b_group,
                                            w_router, b_router, x2, hf, table, weights, wo_raw, wo_loaded)
        x2_ahead = kept.enter_context(nc.sbuf_tensor("x2_ahead", [P, AHEAD, D], F32))
        x2_ahead_loaded = kept.enter_context(nc.semaphore("x2_ahead_loaded"))
        y_weight = experts(nc, kept, ident, rec_all, counts, hf, table, weights, y, x2, x2_ahead, x2_ahead_loaded)
        combine(nc, y_weight, x2, x2_ahead, x2_ahead_loaded, y, final_norm, out)


_INS = ["x", "meta", "norm_mix", "w_in", "conv_w", "conv_b", "conv_ln_g", "conv_ln_b", "w_conv_out", "pool_w", "pool_scale",
        "sc_w", "w_sc_out", "w_out", "norm_ffn", "w_group", "b_group", "w_router", "b_router", "w1", "w3", "w2", "final_norm"]


def kernel(**inputs):
    import numpy as np
    import concourse.bacc as bacc
    from concourse.bass_utils import run_bass_kernel_spmd

    nc = bacc.Bacc("TRN2", target_bir_lowering=False, num_devices=1)
    arrays, args = {}, []
    for name in _INS:
        a = np.ascontiguousarray(inputs[name])
        arrays[f"in_{name}"] = a
        args.append(nc.dram_tensor(f"in_{name}", a.shape, mybir.dt.from_np(a.dtype), kind="ExternalInput").ap())
    out = nc.dram_tensor("out", (1, T, D), F32, kind="ExternalOutput").ap()
    build(nc, *args, out)
    return run_bass_kernel_spmd(nc, [arrays], core_ids=[0]).results[0]["out"]
```
